# Optimizing a Trainium2 kernel written in Bass

```python
import math
import jax
import jax.numpy as jnp
from jax import lax
import numpy as np

D_MODEL = 1024
BATCH = 1
SEQ = 256
DEPTH = 1

GRID_W = 64
CTX_LEN = 256
N_BRANCH = 3
BRANCH_WIDTH = D_MODEL // 2
POOL_WINDOWS = (2, 4, 8, 16)
POOL_GROUPS = len(POOL_WINDOWS)
POOL_GROUP_DIM = BRANCH_WIDTH // POOL_GROUPS
DIFF_HEAD_DIM = 64
DIFF_HEADS = BRANCH_WIDTH // (2 * DIFF_HEAD_DIM)
DIFF_V_DIM = 2 * DIFF_HEAD_DIM
DIFF_QK_WIDTH = DIFF_HEADS * 2 * DIFF_HEAD_DIM
DIFF_V_WIDTH = DIFF_HEADS * DIFF_V_DIM
ROPE_AXIS_FREQS = DIFF_HEAD_DIM // 4
ROPE_THETA = 10000.0
Q_BLOCK = 128
RWKV_HEAD = 64
RWKV_HEADS = BRANCH_WIDTH // RWKV_HEAD
RWKV_WIDTH = RWKV_HEADS * RWKV_HEAD
DECAY_LORA = 64
AAA_LORA = 64
GATE_LORA = 128
RWKV_SPLITS = (RWKV_WIDTH, RWKV_WIDTH, RWKV_WIDTH, 2 * DECAY_LORA, 2 * AAA_LORA, GATE_LORA)
RWKV_IN = 3 * RWKV_WIDTH + 2 * DECAY_LORA + 2 * AAA_LORA + GATE_LORA
IN_SPLITS = (BRANCH_WIDTH, DIFF_QK_WIDTH, DIFF_QK_WIDTH, DIFF_V_WIDTH, RWKV_IN, N_BRANCH * D_MODEL)
IN_WIDTH = BRANCH_WIDTH + 2 * DIFF_QK_WIDTH + DIFF_V_WIDTH + RWKV_IN + N_BRANCH * D_MODEL
N_GROUPS = 4
EXPERTS_PER_GROUP = 8
N_EXPERTS = N_GROUPS * EXPERTS_PER_GROUP
TOP_K = 2
EXPERT_FF = D_MODEL // 2
MOE_BLOCK = 128
N_MOD = 6
NORM_EPS = 1e-6
GN_EPS = 64e-5


def split_cols(p, sizes):
    return jnp.split(p, [int(s) for s in np.cumsum(sizes)[:-1]], axis=-1)

def rms_norm(x, g):
    xf = x.astype(jnp.float32)
    y = xf * lax.rsqrt(jnp.mean(xf * xf, axis=-1, keepdims=True) + NORM_EPS)
    return (y * g.astype(jnp.float32)).astype(x.dtype)

def modulate(x, g, shift, scale):
    return rms_norm(x, g) * (1 + scale) + shift

def centred_window_mean(u, win):
    L = u.shape[1]
    cs = jnp.pad(jnp.cumsum(u.astype(jnp.float32), axis=1), ((0, 0), (1, 0), (0, 0)))
    t = jnp.arange(L)
    lo = jnp.clip(t - win // 2, 0, L - 1)
    hi = jnp.clip(t + win // 2 - 1, 0, L - 1)
    cnt = (hi - lo + 1).astype(jnp.float32)
    return (cs[:, hi + 1] - cs[:, lo]) / cnt[None, :, None]

def pool_mixer(u, w_pool, pool_scale):
    B, L, _ = u.shape
    ug = u.reshape(B, L, POOL_GROUPS, POOL_GROUP_DIM)
    pooled = jnp.stack([centred_window_mean(ug[:, :, i], w) for i, w in enumerate(POOL_WINDOWS)], axis=2)
    diff = pooled.astype(u.dtype) - ug
    y = jnp.einsum('blgc,gcd->blgd', diff, w_pool)
    return y.reshape(B, L, BRANCH_WIDTH) * pool_scale

def rope_rotate(u, ang):
    u1, u2 = jnp.split(u, 2, axis=-1)
    cs = jnp.cos(ang).astype(u.dtype)
    sn = jnp.sin(ang).astype(u.dtype)
    return jnp.concatenate([u1 * cs - u2 * sn, u2 * cs + u1 * sn], axis=-1)

def axial_rope(x, ang_r, ang_c):
    xr, xc = jnp.split(x, 2, axis=-1)
    ar = ang_r[None, :, None, None, :]
    ac = ang_c[None, :, None, None, :]
    return jnp.concatenate([rope_rotate(xr, ar), rope_rotate(xc, ac)], axis=-1)

def diff_qkv(pq, pk, pv, qn_g, kn_g):
    B, L, _ = pq.shape
    q = rms_norm(pq.reshape(B, L, DIFF_HEADS, 2, DIFF_HEAD_DIM), qn_g)
    k = rms_norm(pk.reshape(B, L, DIFF_HEADS, 2, DIFF_HEAD_DIM), kn_g)
    v = pv.reshape(B, L, DIFF_HEADS, DIFF_V_DIM)
    return q, k, v

def diff_attn_block(qb, keys, vals, lam):
    s = jnp.einsum('bqhmd,bkhmd->bhmqk', qb, keys).astype(jnp.float32) * (DIFF_HEAD_DIM ** -0.5)
    p = jax.nn.softmax(s, axis=-1)
    a = p[:, :, 0] - lam * p[:, :, 1]
    return jnp.einsum('bhqk,bkhv->bqhv', a.astype(vals.dtype), vals)

def diff_attn_latent(q, keys, vals, lam):
    B, L = q.shape[:2]
    nb = L // Q_BLOCK
    qb = jnp.moveaxis(q.reshape(B, nb, Q_BLOCK, DIFF_HEADS, 2, DIFF_HEAD_DIM), 1, 0)
    out = lax.map(lambda blk: diff_attn_block(blk, keys, vals, lam), qb)
    return jnp.moveaxis(out, 0, 1).reshape(B, L, DIFF_HEADS, DIFF_V_DIM)

def diff_post(o, subln_g, lam_init):
    B, L = o.shape[:2]
    return (rms_norm(o, subln_g) * (1 - lam_init)).reshape(B, L, DIFF_V_WIDTH)

def token_shift_centred(u, mu):
    prev = jnp.pad(u, ((0, 0), (1, 0), (0, 0)))[:, :-1]
    nxt = jnp.pad(u, ((0, 0), (0, 1), (0, 0)))[:, 1:]
    return u + (prev - u) * mu[0] + (nxt - u) * mu[1]

def rwkv_prepare(pr, shift_mu, w0, w2, a0, a2, g2, k_k, k_a):
    B, L, _ = pr.shape
    u = token_shift_centred(pr, shift_mu)
    r, k, v, wl, al, gl = split_cols(u, RWKV_SPLITS)
    wl = wl.reshape(B, L, 2, DECAY_LORA)
    al = al.reshape(B, L, 2, AAA_LORA)
    w_log = -jax.nn.softplus(-(w0 + jnp.einsum('bldr,drc->bldc', jnp.tanh(wl), w2))) - 0.5
    decay = jnp.exp(-jnp.exp(w_log.astype(jnp.float32)))
    a = jax.nn.sigmoid(a0 + jnp.einsum('bldr,drc->bldc', al, a2))
    g = jax.nn.sigmoid(gl) @ g2
    kk = (k * k_k).reshape(B, L, RWKV_HEADS, RWKV_HEAD).astype(jnp.float32)
    kk = kk / jnp.maximum(jnp.sqrt(jnp.sum(kk * kk, axis=-1, keepdims=True)), 1e-12)
    kk = kk.reshape(B, L, RWKV_WIDTH).astype(k.dtype)
    k_mod = k[:, :, None] * (1 + (a - 1) * k_a)
    b_vec = kk[:, :, None] * a
    return r, k_mod, v, decay, -kk, b_vec, g

def to_scan(u):
    B, L = u.shape[:2]
    u = jnp.stack([u[:, :, 0], jnp.flip(u[:, :, 1], axis=1)], axis=0)
    return jnp.moveaxis(u.reshape(2, B, L, RWKV_HEADS, RWKV_HEAD), 2, 0).astype(jnp.float32)

def wkv_step(S, inp):
    r, w, k, v, a, b = inp
    sa = jnp.einsum('dbhvk,dbhk->dbhv', S, a)
    S = S * w[..., None, :] + sa[..., None] * b[..., None, :] + v[..., None] * k[..., None, :]
    return S, jnp.einsum('dbhvk,dbhk->dbhv', S, r)

def wkv_bidir(S0, r, k_mod, v, decay, a_vec, b_vec):
    B, L, C = r.shape
    both = lambda u: jnp.broadcast_to(u[:, :, None], (B, L, 2, C))
    xs = tuple(to_scan(u) for u in (both(r), decay, k_mod, both(v), both(a_vec), b_vec))
    S, ys = lax.scan(wkv_step, S0, xs)
    y = ys[:, 0] + jnp.flip(ys[:, 1], axis=0)
    return S, jnp.moveaxis(y, 0, 1)

def rwkv_output(y, prep, r_k, gn_w, gn_b):
    r, k_mod, v, g = prep[0], prep[1], prep[2], prep[6]
    B, L, _ = r.shape
    mu = jnp.mean(y, axis=-1, keepdims=True)
    var = jnp.mean(jnp.square(y - mu), axis=-1, keepdims=True)
    yn = ((y - mu) * lax.rsqrt(var + GN_EPS)).reshape(B, L, RWKV_WIDTH) * gn_w + gn_b
    coef = jnp.sum((r[:, :, None] * k_mod * r_k.reshape(-1)).reshape(B, L, 2, RWKV_HEADS, RWKV_HEAD), axis=(2, 4))
    bonus = (coef[..., None] * v.reshape(B, L, RWKV_HEADS, RWKV_HEAD)).reshape(B, L, RWKV_WIDTH)
    return (yn.astype(r.dtype) + bonus) * g

def merge_branches(branches, gates, w_br, w_out):
    B, L, _ = gates.shape
    g = jax.nn.sigmoid(gates.reshape(B, L, N_BRANCH, D_MODEL))
    merged = g[:, :, 0] * (branches[0] @ w_br[0])
    for n in range(1, N_BRANCH):
        merged = merged + g[:, :, n] * (branches[n] @ w_br[n])
    return merged @ w_out

def expert_dispatch(h, eid, gates, w_g, w_u, w_d):
    T, D = h.shape
    A = T * TOP_K
    flat_e = eid.reshape(A)
    flat_tok = jnp.repeat(jnp.arange(T, dtype=jnp.int32), TOP_K)
    order = jnp.argsort(flat_e)
    e_sorted = flat_e[order]
    counts = jnp.bincount(flat_e, length=N_EXPERTS)
    padded = (counts + MOE_BLOCK - 1) // MOE_BLOCK * MOE_BLOCK
    start = jnp.cumsum(counts) - counts
    pend = jnp.cumsum(padded)
    pstart = pend - padded
    slot = pstart[e_sorted] + jnp.arange(A, dtype=jnp.int32) - start[e_sorted]
    P = -(-A // MOE_BLOCK) * MOE_BLOCK + N_EXPERTS * MOE_BLOCK
    n_blk = P // MOE_BLOCK
    slot_tok = jnp.full((P,), T, jnp.int32).at[slot].set(flat_tok[order])
    slot_gate = jnp.zeros((P,), h.dtype).at[slot].set(gates.reshape(A)[order])
    blk_e = jnp.minimum(jnp.searchsorted(pend, jnp.arange(n_blk, dtype=jnp.int32) * MOE_BLOCK, side='right'), N_EXPERTS - 1)
    xb = jnp.concatenate([h, jnp.zeros((1, D), h.dtype)], axis=0)[slot_tok].reshape(n_blk, MOE_BLOCK, D)

    def block_ffn(args):
        xblk, e = args
        return (jax.nn.silu(xblk @ w_g[e]) * (xblk @ w_u[e])) @ w_d[e]

    yb = lax.map(block_ffn, (xb, blk_e)).reshape(P, D)
    return jax.ops.segment_sum(yb * slot_gate[:, None], slot_tok, num_segments=T + 1)[:T]

def hier_moe(h, w_rg, w_re, w_g, w_u, w_d):
    T = h.shape[0]
    lg = (h @ w_rg).astype(jnp.float32)
    grp = jnp.argmax(lg, axis=-1)
    p_grp = jnp.take_along_axis(jax.nn.softmax(lg, axis=-1), grp[:, None], axis=-1)
    le = (h @ w_re).astype(jnp.float32).reshape(T, N_GROUPS, EXPERTS_PER_GROUP)
    le = jnp.take_along_axis(le, grp[:, None, None], axis=1)[:, 0]
    top_v, top_i = lax.top_k(le, TOP_K)
    gates = p_grp * jax.nn.softmax(top_v, axis=-1)
    eid = (grp[:, None] * EXPERTS_PER_GROUP + top_i).astype(jnp.int32)
    return expert_dispatch(h, eid, gates.astype(h.dtype), w_g, w_u, w_d)

def first_inputs(seed: int = 0) -> dict:
    key = jax.random.key(seed)
    keys = jax.random.split(key, 40)
    cnt = [0]

    def nk():
        cnt[0] += 1
        return keys[cnt[0] - 1]

    def nrm(shape, scale):
        return scale * jax.random.normal(nk(), shape, jnp.float32)

    def uni(shape, lo, hi):
        return jax.random.uniform(nk(), shape, jnp.float32, lo, hi)

    D = D_MODEL
    return {
        'x': nrm((BATCH, SEQ, D), 1.0),
        'c': nrm((BATCH, D), 1.0),
        'ctx': nrm((BATCH, CTX_LEN, D), 1.0),
        'c_ctx': nrm((D,), 1.0),
        'w_ada': nrm((DEPTH, D, N_MOD * D), 0.5 * D ** -0.5),
        'b_ada': nrm((DEPTH, N_MOD * D), 0.02),
        'norm1_g': 1.0 + nrm((DEPTH, D), 0.05),
        'norm2_g': 1.0 + nrm((DEPTH, D), 0.05),
        'w_in': nrm((DEPTH, D, IN_WIDTH), D ** -0.5),
        'pool_w': nrm((DEPTH, POOL_GROUPS, POOL_GROUP_DIM, POOL_GROUP_DIM), POOL_GROUP_DIM ** -0.5),
        'pool_scale': 1.0 + nrm((DEPTH, BRANCH_WIDTH), 0.1),
        'q_norm_g': 1.0 + nrm((DEPTH, DIFF_HEAD_DIM), 0.05),
        'k_norm_g': 1.0 + nrm((DEPTH, DIFF_HEAD_DIM), 0.05),
        'lambda_qk': nrm((DEPTH, 4, DIFF_HEAD_DIM), 0.1),
        'subln_g': 1.0 + nrm((DEPTH, DIFF_V_DIM), 0.05),
        'shift_mu': uni((DEPTH, 2, RWKV_IN), 0.0, 0.5),
        'decay_w0': uni((DEPTH, 2, RWKV_WIDTH), -4.0, 1.0),
        'decay_w2': nrm((DEPTH, 2, DECAY_LORA, RWKV_WIDTH), 0.5 * DECAY_LORA ** -0.5),
        'aaa_a0': nrm((DEPTH, 2, RWKV_WIDTH), 0.5),
        'aaa_a2': nrm((DEPTH, 2, AAA_LORA, RWKV_WIDTH), 0.5 * AAA_LORA ** -0.5),
        'gate_w2': nrm((DEPTH, GATE_LORA, RWKV_WIDTH), GATE_LORA ** -0.5),
        'k_k': 0.85 + nrm((DEPTH, RWKV_WIDTH), 0.1),
        'k_a': 1.0 + nrm((DEPTH, RWKV_WIDTH), 0.1),
        'r_k': nrm((DEPTH, RWKV_HEADS, RWKV_HEAD), 0.1),
        'gn_w': 1.0 + nrm((DEPTH, RWKV_WIDTH), 0.05),
        'gn_b': nrm((DEPTH, RWKV_WIDTH), 0.02),
        'w_br': nrm((DEPTH, N_BRANCH, BRANCH_WIDTH, D), BRANCH_WIDTH ** -0.5),
        'w_out': nrm((DEPTH, D, D), D ** -0.5),
        'w_router_group': nrm((DEPTH, D, N_GROUPS), D ** -0.5),
        'w_router_expert': nrm((DEPTH, D, N_EXPERTS), D ** -0.5),
        'w_exp_gate': nrm((DEPTH, N_EXPERTS, D, EXPERT_FF), D ** -0.5),
        'w_exp_up': nrm((DEPTH, N_EXPERTS, D, EXPERT_FF), D ** -0.5),
        'w_exp_down': nrm((DEPTH, N_EXPERTS, EXPERT_FF, D), EXPERT_FF ** -0.5),
    }

def first_block(x, c, ctx, c_ctx, w_ada, b_ada, norm1_g, norm2_g, w_in, pool_w, pool_scale, q_norm_g, k_norm_g,
              lambda_qk, subln_g, shift_mu, decay_w0, decay_w2, aaa_a0, aaa_a2, gate_w2, k_k, k_a, r_k, gn_w, gn_b,
              w_br, w_out, w_router_group, w_router_expert, w_exp_gate, w_exp_up, w_exp_down):
    B, L, D = x.shape
    C = ctx.shape[1]
    rows = L // GRID_W
    row_idx = jnp.repeat(jnp.arange(rows), GRID_W).astype(jnp.float32)
    col_idx = jnp.tile(jnp.arange(GRID_W), rows).astype(jnp.float32)
    inv_freq = ROPE_THETA ** (-jnp.arange(ROPE_AXIS_FREQS, dtype=jnp.float32) / ROPE_AXIS_FREQS)
    ang_r = row_idx[:, None] * inv_freq
    ang_c = col_idx[:, None] * inv_freq
    s_lat = jax.nn.silu(c)
    s_ctx = jax.nn.silu(c_ctx)
    S0 = jnp.zeros((2, B, RWKV_HEADS, RWKV_HEAD, RWKV_HEAD), jnp.float32)

    for l in range(DEPTH):
        last = l == DEPTH - 1
        mod = (s_lat @ w_ada[l] + b_ada[l]).reshape(B, N_MOD, 1, D)
        mod_c = (s_ctx @ w_ada[l] + b_ada[l]).reshape(N_MOD, 1, 1, D)

        p_l = modulate(x, norm1_g[l], mod[:, 0], mod[:, 1]) @ w_in[l]
        p_c = modulate(ctx, norm1_g[l], mod_c[0], mod_c[1]) @ w_in[l]
        pool_l, q_l, k_l, v_l, rw_l, gate_l = split_cols(p_l, IN_SPLITS)
        pool_c, q_c, k_c, v_c, rw_c, gate_c = split_cols(p_c, IN_SPLITS)

        lam_init = 0.8 - 0.6 * math.exp(-0.3 * l)
        lq = lambda_qk[l].astype(jnp.float32)
        lam = jnp.exp(jnp.sum(lq[0] * lq[1])) - jnp.exp(jnp.sum(lq[2] * lq[3])) + lam_init
        qh_l, kh_l, vh_l = diff_qkv(q_l, k_l, v_l, q_norm_g[l], k_norm_g[l])
        qh_l = axial_rope(qh_l, ang_r, ang_c)
        kh_l = axial_rope(kh_l, ang_r, ang_c)
        qh_c, kh_c, vh_c = diff_qkv(q_c, k_c, v_c, q_norm_g[l], k_norm_g[l])
        keys = jnp.concatenate([kh_c, kh_l], axis=1)
        vals = jnp.concatenate([vh_c, vh_l], axis=1)
        att_l = diff_post(diff_attn_latent(qh_l, keys, vals, lam), subln_g[l], lam_init)

        rw_par = (shift_mu[l], decay_w0[l], decay_w2[l], aaa_a0[l], aaa_a2[l], gate_w2[l], k_k[l], k_a[l])
        prep_c = rwkv_prepare(rw_c, *rw_par)
        S_c, y_c = wkv_bidir(S0, *prep_c[:6])
        prep_l = rwkv_prepare(rw_l, *rw_par)
        _, y_l = wkv_bidir(S_c, *prep_l[:6])
        rwo_l = rwkv_output(y_l, prep_l, r_k[l], gn_w[l], gn_b[l])

        mix_l = merge_branches((pool_mixer(pool_l, pool_w[l], pool_scale[l]), att_l, rwo_l), gate_l, w_br[l], w_out[l])
        x = x + mod[:, 2] * mix_l
        if not last:
            att_c = diff_post(diff_attn_block(qh_c, kh_c, vh_c, lam), subln_g[l], lam_init)
            rwo_c = rwkv_output(y_c, prep_c, r_k[l], gn_w[l], gn_b[l])
            mix_c = merge_branches((pool_mixer(pool_c, pool_w[l], pool_scale[l]), att_c, rwo_c), gate_c, w_br[l], w_out[l])
            ctx = ctx + mod_c[2] * mix_c

        moe_par = (w_router_group[l], w_router_expert[l], w_exp_gate[l], w_exp_up[l], w_exp_down[l])
        f_l = modulate(x, norm2_g[l], mod[:, 3], mod[:, 4]).reshape(B * L, D)
        if last:
            x = x + mod[:, 5] * hier_moe(f_l, *moe_par).reshape(B, L, D)
        else:
            f_c = modulate(ctx, norm2_g[l], mod_c[3], mod_c[4]).reshape(B * C, D)
            y = hier_moe(jnp.concatenate([f_c, f_l], axis=0), *moe_par)
            ctx = ctx + mod_c[5] * y[:B * C].reshape(B, C, D)
            x = x + mod[:, 5] * y[B * C:].reshape(B, L, D)
    return x


DEPTH_2 = 2

HEAD_DIM = 64
ROPE_BASE = 10000.0
EPS = 1e-6
NEG_INF = -1e30

MLA_HEADS = 8
MLA_NOPE = 64
MLA_ROPE = 32
MLA_V = 64
MLA_Q_RANK = 256
MLA_KV_RANK = 128
MLA_IN = MLA_Q_RANK + MLA_KV_RANK + MLA_ROPE

NA_HEADS = 8
NA_KR_MAX = 8
NA_KC = 16
NA_CB = 16
NA_KB = 2 * NA_KC

SWA_HEADS = 16
SWA_KV_HEADS = 2
SWA_WINDOW = 128
SWA_BLOCK = 128

D_FF = (-(-8 * D_MODEL // 3) + 255) // 256 * 256

EVEN_IN = MLA_IN + 3 * NA_HEADS * HEAD_DIM
EVEN_OUT = MLA_HEADS * MLA_V + NA_HEADS * HEAD_DIM
ODD_IN = (SWA_HEADS + 2 * SWA_KV_HEADS) * HEAD_DIM
ODD_OUT = SWA_HEADS * HEAD_DIM
N_EVEN = (DEPTH_2 + 1) // 2
N_ODD = DEPTH_2 // 2


def rms_norm_2(x, gain=None):
    xf = x.astype(jnp.float32)
    y = xf * lax.rsqrt(jnp.mean(xf * xf, axis=-1, keepdims=True) + EPS)
    if gain is not None:
        y = y * gain.astype(jnp.float32)
    return y.astype(x.dtype)

def modulate_2(x, shift, scale):
    return rms_norm_2(x) * (1 + scale) + shift

def axial_rope_2(x, rows, cols):
    half = x.shape[-1] // 2
    inv = ROPE_BASE ** (-jnp.arange(0, half, 2, dtype=jnp.float32) / half)

    def rot(xa, pos):
        ang = pos.astype(jnp.float32)[:, None] * inv
        cos = jnp.cos(ang)[None, :, None, :]
        sin = jnp.sin(ang)[None, :, None, :]
        x1, x2 = jnp.split(xa.astype(jnp.float32), 2, axis=-1)
        return jnp.concatenate([x1 * cos - x2 * sin, x1 * sin + x2 * cos], axis=-1)

    xr, xc = jnp.split(x, 2, axis=-1)
    return jnp.concatenate([rot(xr, rows), rot(xc, cols)], axis=-1).astype(x.dtype)

def swiglu(h, w_gate_up, w_down):
    g, u = jnp.split(h @ w_gate_up, 2, axis=-1)
    return (jax.nn.silu(g) * u) @ w_down

def mla_heads(p_lat, p_ctx, rows, cols, q_norm, kv_norm, w_q_up, w_uk, w_uv, ctx_out):
    b, s = p_lat.shape[:2]
    n_ctx = p_ctx.shape[1]
    scale = (MLA_NOPE + MLA_ROPE) ** -0.5

    def queries(p, rotate):
        q = rms_norm_2(p[..., :MLA_Q_RANK], q_norm) @ w_q_up
        q = q.reshape(p.shape[0], p.shape[1], MLA_HEADS, MLA_NOPE + MLA_ROPE)
        q_nope, q_rope = q[..., :MLA_NOPE], q[..., MLA_NOPE:]
        if rotate:
            q_rope = axial_rope_2(q_rope, rows, cols)
        return jnp.einsum('bshn,hcn->bshc', q_nope, w_uk), q_rope

    def keys(p, rotate):
        c_kv = rms_norm_2(p[..., MLA_Q_RANK:MLA_Q_RANK + MLA_KV_RANK], kv_norm)
        k_rope = p[..., MLA_Q_RANK + MLA_KV_RANK:][:, :, None, :]
        if rotate:
            k_rope = axial_rope_2(k_rope, rows, cols)
        return c_kv, k_rope[:, :, 0]

    def attend(q_lat, q_rope, c_kv, k_rope):
        sc = jnp.einsum('bqhc,bkc->bhqk', q_lat, c_kv) + jnp.einsum('bqhr,bkr->bhqk', q_rope, k_rope)
        p = jax.nn.softmax(sc.astype(jnp.float32) * scale, axis=-1).astype(c_kv.dtype)
        return jnp.einsum('bhqk,bkc->bqhc', p, c_kv)

    ckv_c, kr_c = keys(p_ctx, False)
    ckv_l, kr_l = keys(p_lat, True)
    ckv_all = jnp.concatenate([ckv_c, ckv_l], axis=1)
    kr_all = jnp.concatenate([kr_c, kr_l], axis=1)
    ql, qr = queries(p_lat, True)
    nb = s // Q_BLOCK

    def to_blocks(t):
        return t.reshape(b, nb, Q_BLOCK, *t.shape[2:]).swapaxes(0, 1)

    o = lax.map(lambda a: attend(a[0], a[1], ckv_all, kr_all), (to_blocks(ql), to_blocks(qr)))
    o = o.swapaxes(0, 1).reshape(b, s, MLA_HEADS, MLA_KV_RANK)
    o_lat = jnp.einsum('bshc,hcv->bshv', o, w_uv).reshape(b, s, MLA_HEADS * MLA_V)
    o_ctx = None
    if ctx_out:
        qlc, qrc = queries(p_ctx, False)
        oc = attend(qlc, qrc, ckv_c, kr_c)
        o_ctx = jnp.einsum('bshc,hcv->bshv', oc, w_uv).reshape(b, n_ctx, MLA_HEADS * MLA_V)
    return o_lat, o_ctx

def na_heads(q, k, v, qc, kc, vc, rel_bias, ctx_out):
    b, s, h, d = q.shape
    n_ctx = kc.shape[1]
    n_rows = s // GRID_W
    kr = min(NA_KR_MAX, n_rows)
    n_cb = GRID_W // NA_CB
    scale = d ** -0.5
    qcol = np.arange(GRID_W).reshape(n_cb, NA_CB)
    q_start = np.clip(qcol - NA_KC // 2, 0, GRID_W - NA_KC)
    kb_start = np.clip(np.arange(n_cb) * NA_CB - NA_KC // 2, 0, GRID_W - NA_KB)
    kcol = kb_start[:, None] + np.arange(NA_KB)
    col_ok = (kcol[:, None, :] >= q_start[..., None]) & (kcol[:, None, :] < q_start[..., None] + NA_KC)
    dc_idx = np.clip(kcol[:, None, :] - qcol[..., None] + NA_KC - 1, 0, 2 * NA_KC - 2)
    col_bias = rel_bias[:, :, dc_idx].astype(jnp.float32)
    kg = k.reshape(b, n_rows, GRID_W, h, d)
    vg = v.reshape(b, n_rows, GRID_W, h, d)
    q_rows = q.reshape(b, n_rows, n_cb, NA_CB, h, d).swapaxes(0, 1)

    def row(args):
        r, qr = args
        rs = jnp.clip(r - kr // 2, 0, n_rows - kr)
        k_blk = lax.dynamic_slice_in_dim(kg, rs, kr, axis=1)[:, :, kcol]
        v_blk = lax.dynamic_slice_in_dim(vg, rs, kr, axis=1)[:, :, kcol]
        s_lat = jnp.einsum('bnqhd,bknmhd->bhnqkm', qr, k_blk).astype(jnp.float32) * scale
        dr_idx = rs + jnp.arange(kr) - r + NA_KR_MAX - 1
        s_lat = s_lat + col_bias[:, dr_idx].transpose(0, 2, 3, 1, 4)[None]
        s_lat = jnp.where(col_ok[:, :, None, :], s_lat, NEG_INF).reshape(b, h, n_cb, NA_CB, kr * NA_KB)
        s_ctx = jnp.einsum('bnqhd,bchd->bhnqc', qr, kc).astype(jnp.float32) * scale
        p = jax.nn.softmax(jnp.concatenate([s_ctx, s_lat], axis=-1), axis=-1).astype(v.dtype)
        p_lat = p[..., n_ctx:].reshape(b, h, n_cb, NA_CB, kr, NA_KB)
        return (jnp.einsum('bhnqc,bchd->bnqhd', p[..., :n_ctx], vc)
                + jnp.einsum('bhnqkm,bknmhd->bnqhd', p_lat, v_blk))

    o = lax.map(row, (jnp.arange(n_rows), q_rows))
    o_lat = o.swapaxes(0, 1).reshape(b, s, h * d)
    o_ctx = None
    if ctx_out:
        sc = jnp.einsum('bqhd,bkhd->bhqk', qc, kc).astype(jnp.float32) * scale
        pc = jax.nn.softmax(sc, axis=-1).astype(vc.dtype)
        o_ctx = jnp.einsum('bhqk,bkhd->bqhd', pc, vc).reshape(b, n_ctx, h * d)
    return o_lat, o_ctx

def swa_heads(q, k, v, qc, kc, vc, sinks, ctx_out):
    b, s, h, d = q.shape
    kvh = k.shape[2]
    g = h // kvh
    n_ctx = kc.shape[1]
    scale = d ** -0.5
    nb = s // SWA_BLOCK
    n_side = -(-SWA_WINDOW // SWA_BLOCK)
    pad = n_side * SWA_BLOCK
    kw = (2 * n_side + 1) * SWA_BLOCK

    def windows(t):
        tp = jnp.pad(t, ((0, 0), (pad, pad), (0, 0), (0, 0))).reshape(b, nb + 2 * n_side, SWA_BLOCK, kvh, d)
        return jnp.concatenate([tp[:, j:j + nb] for j in range(2 * n_side + 1)], axis=2).swapaxes(0, 1)

    q_pos = jnp.arange(s).reshape(nb, SWA_BLOCK)
    k_pos = (jnp.arange(nb)[:, None] - n_side) * SWA_BLOCK + jnp.arange(kw)[None, :]
    sink_col = sinks.astype(jnp.float32).reshape(kvh, g, 1, 1)

    def attend(qb, kb, vb, band_ok):
        tq = qb.shape[1]
        qg = qb.reshape(b, tq, kvh, g, d)
        s_ctx = jnp.einsum('bqkgd,bckd->bkgqc', qg, kc).astype(jnp.float32) * scale
        parts = [jnp.broadcast_to(sink_col, (b, kvh, g, tq, 1)), s_ctx]
        if kb is not None:
            s_lat = jnp.einsum('bqkgd,bmkd->bkgqm', qg, kb).astype(jnp.float32) * scale
            parts.append(jnp.where(band_ok, s_lat, NEG_INF))
        p = jax.nn.softmax(jnp.concatenate(parts, axis=-1), axis=-1).astype(vc.dtype)
        o = jnp.einsum('bkgqc,bckd->bqkgd', p[..., 1:1 + n_ctx], vc)
        if kb is not None:
            o = o + jnp.einsum('bkgqm,bmkd->bqkgd', p[..., 1 + n_ctx:], vb)
        return o.reshape(b, tq, h * d)

    def block(args):
        qb, kb, vb, qp, kp = args
        ok = (jnp.abs(kp[None, :] - qp[:, None]) <= SWA_WINDOW) & (kp >= 0)[None, :] & (kp < s)[None, :]
        return attend(qb, kb, vb, ok)

    q_blocks = q.reshape(b, nb, SWA_BLOCK, h, d).swapaxes(0, 1)
    o = lax.map(block, (q_blocks, windows(k), windows(v), q_pos, k_pos))
    o_lat = o.swapaxes(0, 1).reshape(b, s, h * d)
    o_ctx = attend(qc, None, None, None) if ctx_out else None
    return o_lat, o_ctx

def even_mixer(a_lat, a_ctx, rows, cols, w_in, q_norm, kv_norm, w_q_up, w_uk, w_uv, rel_bias, w_out, ctx_out):
    b, s, _ = a_lat.shape
    n_ctx = a_ctx.shape[1]
    p_lat = a_lat @ w_in
    p_ctx = a_ctx @ w_in
    o_mla_lat, o_mla_ctx = mla_heads(p_lat[..., :MLA_IN], p_ctx[..., :MLA_IN], rows, cols,
                                     q_norm, kv_norm, w_q_up, w_uk, w_uv, ctx_out)
    na_l = p_lat[..., MLA_IN:].reshape(b, s, 3, NA_HEADS, HEAD_DIM)
    na_c = p_ctx[..., MLA_IN:].reshape(b, n_ctx, 3, NA_HEADS, HEAD_DIM)
    o_na_lat, o_na_ctx = na_heads(na_l[:, :, 0], na_l[:, :, 1], na_l[:, :, 2],
                                  na_c[:, :, 0], na_c[:, :, 1], na_c[:, :, 2], rel_bias, ctx_out)
    o_lat = jnp.concatenate([o_mla_lat, o_na_lat], axis=-1) @ w_out
    o_ctx = jnp.concatenate([o_mla_ctx, o_na_ctx], axis=-1) @ w_out if ctx_out else None
    return o_lat, o_ctx

def odd_mixer(a_lat, a_ctx, rows, cols, w_in, sinks, w_out, ctx_out):
    b, s, _ = a_lat.shape
    n_ctx = a_ctx.shape[1]

    def split(p, t):
        q = p[..., :SWA_HEADS * HEAD_DIM].reshape(b, t, SWA_HEADS, HEAD_DIM)
        kv = p[..., SWA_HEADS * HEAD_DIM:].reshape(b, t, 2, SWA_KV_HEADS, HEAD_DIM)
        return q, kv[:, :, 0], kv[:, :, 1]

    q, k, v = split(a_lat @ w_in, s)
    q = axial_rope_2(q, rows, cols)
    k = axial_rope_2(k, rows, cols)
    qc, kc, vc = split(a_ctx @ w_in, n_ctx)
    o_lat, o_ctx = swa_heads(q, k, v, qc, kc, vc, sinks, ctx_out)
    return o_lat @ w_out, (o_ctx @ w_out if ctx_out else None)

def second_inputs(seed: int = 0) -> dict:
    key = jax.random.key(seed)
    ks = jax.random.split(key, 20)
    nrm = jax.random.normal
    f32 = jnp.float32
    return {
        'x': nrm(ks[0], (BATCH, SEQ, D_MODEL), f32),
        'c': nrm(ks[1], (BATCH, D_MODEL), f32),
        'ctx': nrm(ks[2], (BATCH, CTX_LEN, D_MODEL), f32),
        'c_ctx': nrm(ks[3], (D_MODEL,), f32),
        'mod_w': nrm(ks[4], (DEPTH_2, D_MODEL, 6 * D_MODEL), f32) * (0.5 * D_MODEL ** -0.5),
        'mod_b': nrm(ks[5], (DEPTH_2, 6 * D_MODEL), f32) * 0.02,
        'even_w_in': nrm(ks[6], (N_EVEN, D_MODEL, EVEN_IN), f32) * D_MODEL ** -0.5,
        'mla_q_norm': 1.0 + 0.02 * nrm(ks[7], (N_EVEN, MLA_Q_RANK), f32),
        'mla_kv_norm': 1.0 + 0.02 * nrm(ks[8], (N_EVEN, MLA_KV_RANK), f32),
        'mla_w_q_up': nrm(ks[9], (N_EVEN, MLA_Q_RANK, MLA_HEADS * (MLA_NOPE + MLA_ROPE)), f32) * MLA_Q_RANK ** -0.5,
        'mla_w_uk': nrm(ks[10], (N_EVEN, MLA_HEADS, MLA_KV_RANK, MLA_NOPE), f32) * MLA_NOPE ** -0.5,
        'mla_w_uv': nrm(ks[11], (N_EVEN, MLA_HEADS, MLA_KV_RANK, MLA_V), f32) * MLA_KV_RANK ** -0.5,
        'na_rel_bias': 0.2 * nrm(ks[12], (N_EVEN, NA_HEADS, 2 * NA_KR_MAX - 1, 2 * NA_KC - 1), f32),
        'even_w_out': nrm(ks[13], (N_EVEN, EVEN_OUT, D_MODEL), f32) * EVEN_OUT ** -0.5,
        'odd_w_in': nrm(ks[14], (N_ODD, D_MODEL, ODD_IN), f32) * D_MODEL ** -0.5,
        'swa_sinks': nrm(ks[15], (N_ODD, SWA_HEADS), f32),
        'odd_w_out': nrm(ks[16], (N_ODD, ODD_OUT, D_MODEL), f32) * ODD_OUT ** -0.5,
        'ffn_w_gate_up': nrm(ks[17], (DEPTH_2, D_MODEL, 2 * D_FF), f32) * D_MODEL ** -0.5,
        'ffn_w_down': nrm(ks[18], (DEPTH_2, D_FF, D_MODEL), f32) * D_FF ** -0.5,
        'final_norm': 1.0 + 0.02 * nrm(ks[19], (D_MODEL,), f32),
    }

def second_block(x, c, ctx, c_ctx, mod_w, mod_b, even_w_in, mla_q_norm, mla_kv_norm, mla_w_q_up, mla_w_uk,
              mla_w_uv, na_rel_bias, even_w_out, odd_w_in, swa_sinks, odd_w_out, ffn_w_gate_up, ffn_w_down,
              final_norm):
    s = x.shape[1]
    t = jnp.arange(s, dtype=jnp.int32)
    rows, cols = t // GRID_W, t % GRID_W
    h_lat, h_ctx = x, ctx
    silu_c = jax.nn.silu(c)[:, None, :]
    silu_cc = jax.nn.silu(c_ctx)[None, None, :]
    for l in range(DEPTH_2):
        ctx_out = l < DEPTH_2 - 1
        sh_a, sc_a, g_a, sh_f, sc_f, g_f = jnp.split(silu_c @ mod_w[l] + mod_b[l], 6, axis=-1)
        csh_a, csc_a, cg_a, csh_f, csc_f, cg_f = jnp.split(silu_cc @ mod_w[l] + mod_b[l], 6, axis=-1)
        a_lat = modulate_2(h_lat, sh_a, sc_a)
        a_ctx = modulate_2(h_ctx, csh_a, csc_a)
        if l % 2 == 0:
            e = l // 2
            o_lat, o_ctx = even_mixer(a_lat, a_ctx, rows, cols, even_w_in[e], mla_q_norm[e], mla_kv_norm[e],
                                      mla_w_q_up[e], mla_w_uk[e], mla_w_uv[e], na_rel_bias[e], even_w_out[e],
                                      ctx_out)
        else:
            o = l // 2
            o_lat, o_ctx = odd_mixer(a_lat, a_ctx, rows, cols, odd_w_in[o], swa_sinks[o], odd_w_out[o], ctx_out)
        h_lat = h_lat + g_a * o_lat
        h_lat = h_lat + g_f * swiglu(modulate_2(h_lat, sh_f, sc_f), ffn_w_gate_up[l], ffn_w_down[l])
        if ctx_out:
            h_ctx = h_ctx + cg_a * o_ctx
            h_ctx = h_ctx + cg_f * swiglu(modulate_2(h_ctx, csh_f, csc_f), ffn_w_gate_up[l], ffn_w_down[l])
    return rms_norm_2(h_lat, final_norm)


def setup_inputs(seed=0):
    out = dict(first_inputs(seed))
    for name, value in second_inputs(seed + 1).items():
        if name != "x":
            out[name + "_2"] = value
    return out


def reference(
    x, c, ctx, c_ctx, w_ada, b_ada, norm1_g, norm2_g, w_in, pool_w, pool_scale, q_norm_g,
    k_norm_g, lambda_qk, subln_g, shift_mu, decay_w0, decay_w2, aaa_a0, aaa_a2, gate_w2, k_k,
    k_a, r_k, gn_w, gn_b, w_br, w_out, w_router_group, w_router_expert, w_exp_gate, w_exp_up,
    w_exp_down, c_2, ctx_2, c_ctx_2, mod_w_2, mod_b_2, even_w_in_2, mla_q_norm_2, mla_kv_norm_2,
    mla_w_q_up_2, mla_w_uk_2, mla_w_uv_2, na_rel_bias_2, even_w_out_2, odd_w_in_2, swa_sinks_2,
    odd_w_out_2, ffn_w_gate_up_2, ffn_w_down_2, final_norm_2,
):
    x = first_block(
        x, c, ctx, c_ctx, w_ada, b_ada, norm1_g, norm2_g, w_in, pool_w, pool_scale, q_norm_g,
        k_norm_g, lambda_qk, subln_g, shift_mu, decay_w0, decay_w2, aaa_a0, aaa_a2, gate_w2,
        k_k, k_a, r_k, gn_w, gn_b, w_br, w_out, w_router_group, w_router_expert, w_exp_gate,
        w_exp_up, w_exp_down,
    )
    return second_block(
        x, c_2, ctx_2, c_ctx_2, mod_w_2, mod_b_2, even_w_in_2, mla_q_norm_2, mla_kv_norm_2,
        mla_w_q_up_2, mla_w_uk_2, mla_w_uv_2, na_rel_bias_2, even_w_out_2, odd_w_in_2,
        swa_sinks_2, odd_w_out_2, ffn_w_gate_up_2, ffn_w_down_2, final_norm_2,
    )


_drawn_inputs = setup_inputs


def setup_inputs(seed=0):
    import zlib

    import numpy as np

    out = dict(_drawn_inputs(seed))
    spreads = {}
    factors = {'norm1_g': 2.801,
     'pool_scale': 2.903,
     'q_norm_g': 6.383,
     'k_norm_g': 5.819,
     'lambda_qk': 8.0,
     'subln_g': 4.424,
     'decay_w2': 4.473,
     'aaa_a2': 3.102,
     'k_k': 3.183,
     'gn_w': 6.814,
     'gn_b': 7.977,
     'mla_q_norm_2': 8.0,
     'mla_kv_norm_2': 8.0,
     'na_rel_bias_2': 28.394,
     'swa_sinks_2': 56.404}
    for name, (base, spread) in spreads.items():
        noise = np.random.default_rng([zlib.crc32(name.encode()), seed]).standard_normal(out[name].shape)
        drawn = base * np.exp(spread * noise) if base else spread * noise
        out[name] = jnp.asarray(drawn.astype(out[name].dtype))
    for name, factor in factors.items():
        out[name] = (out[name] * factor).astype(out[name].dtype)
    return out
```

```python
import math
from contextlib import ExitStack

import numpy as np

import concourse.bass as bass
from concourse import mybir

F32 = mybir.dt.float32
U32 = mybir.dt.uint32
I32 = mybir.dt.int32
ALU = mybir.AluOpType
ACT = mybir.ActivationFunctionType
AX = mybir.AxisListType.X

P = 128
D = 1024
KD = D // P
SEQ = 256
CTX = 256
T = CTX + SEQ
LAT = slice(CTX, T)
GRID_W = 64
EPS = 1e-6
GN_EPS = 64e-5
BW = 512
JT = BW // P
CH = 64
NCH = T // CH
NE, NG, EPG = 32, 4, 8
SLOTS = 64
FF = 2816
FT = FF // P
NRW = 15
RW_R, RW_K, RW_V, RW_W, RW_A, RW_G = 0, 4, 8, 12, 13, 14
LAM_INIT = 0.8 - 0.6 * math.exp(0.0)
POOL_WINDOWS = (2, 4, 8, 16)
NEG = -1e30

TILE = 2048
UPT = TILE // P
RING = 6
EXP_TILES = 6
ROUTES = 2 * SEQ
ITEMS = (ROUTES + NE * (SLOTS - 1)) // SLOTS
ITEMS += ITEMS % 2
PAIR = 2 * SLOTS
BODY = 2 * EXP_TILES


def _rope(half, lanes):
    freqs = half // 2
    inv = (np.float32(10000.0) ** (-np.arange(freqs, dtype=np.float32) / np.float32(freqs))).astype(np.float32)
    t = np.arange(SEQ)
    pos = [(t // GRID_W).astype(np.float32), (t % GRID_W).astype(np.float32)]
    cos, sin = np.zeros((P, SEQ), np.float32), np.zeros((P, SEQ), np.float32)
    perm = np.zeros((P, P), np.float32)
    for p in range(P):
        i = p % lanes
        axis, r = i // half, i % half
        ang = pos[axis] * inv[r % freqs]
        cos[p] = np.cos(ang)
        sin[p] = np.sin(ang) * (-1.0 if r < freqs else 1.0)
        perm[p + freqs if r < freqs else p - freqs, p] = 1.0
    return cos, sin, perm


def constants():
    eye = np.eye(P, dtype=np.float32)
    i, j = np.arange(P)[:, None], np.arange(P)[None, :]
    c = {}
    c["ident"] = eye
    c["ones"] = np.ones((P, P), np.float32)
    c["blk"] = (i // 64 == j // 64).astype(np.float32)
    c["cos64"], c["sin64"], c["perm64"] = _rope(32, 64)
    c["cos32"], c["sin32"], c["perm32"] = _rope(16, 32)
    c["restart"] = np.tile((np.arange(T) % CH != 0).astype(np.float32), (P, 1))
    a, b = (np.arange(P) % 64)[:, None], np.arange(64)[None, :]
    bd = (a // 32 == b // 32)
    for d in range(2):
        before = a < b if d == 0 else a > b
        upto = a <= b if d == 0 else a >= b
        after = a > b if d == 0 else a < b
        c[f"mB{d}"] = np.concatenate([before & bd, upto], 1).astype(np.float32)
        c[f"mK{d}"] = np.concatenate([before, upto], 1).astype(np.float32)
        c[f"mA{d}"] = np.concatenate([after & bd, after & ~bd], 1).astype(np.float32)
    c["eye64"] = (a == b).astype(np.float32)
    c["tri"] = (i < j).astype(np.float32)
    c["iota"] = np.tile(np.arange(SLOTS, dtype=np.float32), (P, 1))
    q, k = np.arange(SEQ)[:, None], np.arange(SEQ)[None, :]
    far = np.where(np.abs(q - k) <= 128, 0.0, NEG).astype(np.float32)
    c["swa"] = np.concatenate([far[:P], far[P:]], 1)
    c["number"] = np.arange(P, dtype=np.float32)[:, None]
    c["band"] = (np.arange(P)[:, None] // 32 == np.arange(4)[None, :]).astype(np.float32)
    cnt = []
    for w in POOL_WINDOWS:
        lo = np.clip(np.arange(SEQ) - w // 2, 0, SEQ - 1)
        hi = np.clip(np.arange(SEQ) + w // 2 - 1, 0, SEQ - 1)
        cnt.append(1.0 / (hi - lo + 1))
    c["cnt"] = np.tile(np.concatenate(cnt).astype(np.float32), (P, 1))
    return c


def offsets(widths):
    out, at = {}, 0
    for name, w in widths:
        out[name] = (at, w)
        at += w
    return out, at


LATE = ("cnt", "swa")
CONST_WIDTHS = [(n, v.shape[1]) for n, v in constants().items() if n not in LATE]
CONST_AT, CONST_W = offsets(CONST_WIDTHS)

PARAM_WIDTHS = [
    ("c1", 16), ("c2", 16), ("b_ada", 96), ("mod_b0", 96), ("mod_b1", 96), ("norm1_g", 8), ("norm2_g", 8),
    ("pool_scale", 4), ("q_norm_g", 1), ("k_norm_g", 1), ("subln_g", 1), ("mu0", 15), ("mu1", 15),
    ("w0", 8), ("a0", 8), ("k_k", 4), ("k_a", 4), ("r_k", 4), ("gn_w", 4), ("gn_b", 4),
    ("mla_q_norm", 2), ("mla_kv_norm", 1), ("final_norm", 8), ("sinks", 16),
]
PARAM_AT, PARAM_W = offsets(PARAM_WIDTHS)
SW1_AT, SW1_W = offsets([("pool_w", 512), ("w2", 512), ("a2", 512), ("g2", 512), ("router", KD * 36)])
SW2_AT, SW2_W = offsets([("q_up", 2 * 768), ("uk", 512), ("uv", 512)])
SW_W = max(SW1_W, SW2_W)

N_ADA = 48 * KD
N_QKVP = 12 * KD + 32
N_RW = NRW * KD + KD
N_MERGE = KD * 3 * (KD + JT)
N_OUT = KD * KD
N_EVEN = 12 * KD + 32
N_FFN = FT * 2 * KD + KD * FT
N_ODD = 10 * KD
PRE = (3 * N_ADA + N_QKVP + N_RW + N_MERGE + N_OUT) // UPT
POST = (N_EVEN + N_OUT + N_FFN + N_ODD + N_OUT + N_FFN) // UPT
ADA = N_ADA // UPT
N_TILES = PRE + EXP_TILES * ITEMS + POST
for _n in (N_ADA, N_QKVP, N_RW, N_MERGE, N_OUT, N_EVEN, N_FFN, N_ODD):
    assert _n % UPT == 0

ARENA = 25344


class Side:

    def __init__(self, nc, eng, name, full, back, chain, reads, named):
        self.nc, self.eng, self.name = nc, eng, name
        self.full, self.back, self.chain = full, back, chain
        self.reads, self.named = reads, named
        self.n_back = self.n_chain = self.n_read = 0
        self.own = {}
        self.base, self.it, self.step = {}, None, {}

    def at(self, key, value):
        if self.it is None or key not in self.step:
            return value
        return value + self.it * self.step[key]

    def take(self):
        bank, n = self.reads[self.n_read]
        self.n_read += 1
        self.eng.wait_ge(self.full, self.at("full", n))
        return bank

    def gives(self, ins):
        ins.then_inc(self.back, 1)
        self.n_back += 1
        self.eng.wait_ge(self.back, self.at("back_" + self.name, self.n_back))

    def given(self, ins):
        ins.then_inc(self.back, 1)
        self.n_back += 1

    def does(self, ins):
        ins.then_inc(self.chain, 1)
        self.n_chain += 1
        self.eng.wait_ge(self.chain, self.at("chain_" + self.name, self.n_chain))

    def signals(self, ins, name):
        sem = self.named(name)
        ins.then_inc(sem, 1)
        self.own[name] = self.own.get(name, 0) + 1
        self.eng.wait_ge(sem, self.at(name, self.own[name]))


def build(nc, dram, out):
    with ExitStack() as ctx:
        def sb(name, cols, dt=F32):
            return ctx.enter_context(nc.sbuf_tensor(name, [P, cols], dt))

        sems = {}

        def S(name):
            if name not in sems:
                sems[name] = ctx.enter_context(nc.semaphore(name))
            return sems[name]

        ring = sb("ring", RING * TILE)
        Ht = sb("resid", KD * T)
        At = sb("normed", KD * T)
        par = sb("par", PARAM_W)
        con = sb("con", CONST_W)
        sw = sb("sw", SW_W)
        mod1 = sb("mod1", 96)
        mod2a = sb("mod2a", 96)
        mod2b = sb("mod2b", 96)
        coef = sb("coef", 32)
        rs_t = sb("rs_t", T)
        arena = sb("arena", ARENA)
        small = sb("small", 160)
        item_expert = sb("item_expert", ITEMS, I32)
        idx = sb("idx", 32, U32)
        eps_c = sb("eps_c", 2)
        tots_t = sb("tots", 64)
        tots = tots_t[:, :].rearrange("p (x c) -> p x c", x=8)
        MX, LM, GNC = 64, 80, 96
        neglam = small[:, LM + 4:LM + 5]
        c0t = small[:, 128:143]
        oneka = small[:, 144:148]
        banks = [ctx.enter_context(nc.psum_tensor(f"bank{i}", [P, 512], F32)) for i in range(8)]

        H = Ht[:, :].rearrange("p (k t) -> p k t", k=KD)
        A = At[:, :].rearrange("p (k t) -> p k t", k=KD)

        def C(name):
            o, w = CONST_AT[name]
            return con[:, o:o + w]

        def Q(name, i=0, n=1):
            o, w = PARAM_AT[name]
            return par[:, o + i:o + i + n]

        def region(base, cols, pattern=None, **kw):
            v = arena[:, base:base + cols]
            return v.rearrange(pattern, **kw) if pattern else v

        id2 = C("eye64")
        ident, ones, blk = C("ident"), C("ones"), C("blk")
        sw1 = {n: sw[:, o:o + w] for n, (o, w) in SW1_AT.items()}
        sw2 = {n: sw[:, o:o + w] for n, (o, w) in SW2_AT.items()}

        full, chain = S("product_complete"), {n: S(f"{n}_step") for n in ("act", "dve")}
        back = {n: S(f"{n}_gave_back") for n in ("act", "dve")}
        ring_full = [S(f"weights_in_{i}") for i in range(RING)]
        reads = {"act": [], "dve": []}
        tile_free = []
        act_s = Side(nc, nc.scalar, "act", full, back["act"], chain["act"], reads["act"], S)
        dve_s = Side(nc, nc.vector, "dve", full, back["dve"], chain["dve"], reads["dve"], S)

        cond1 = region(0, KD * 32, "p (k n) -> p k n", k=KD)
        cond2 = A[:, 4, 0:CTX].rearrange("p (k n) -> p k n", k=KD)
        pool_in = region(0, 1024, "p (j t) -> p j t", j=JT)
        q_in = region(1024, 1024, "p (j t) -> p j t", j=JT)
        k_in = region(2048, 2048, "p (j t) -> p j t", j=JT)
        v_in = region(4096, 2048, "p (i n) -> p i n", i=4)
        att_out = H[:, 0:4, 0:CTX]
        pool_out = H[:, 4:8, 0:CTX]
        w1a = region(6144, 1024, "p (j t) -> p j t", j=JT)
        w1b = region(7168, 1024, "p (j t) -> p j t", j=JT)
        ATT = 8192
        xtok = region(ATT, 4096, "p (i n) -> p i n", i=4)
        sq_t = region(ATT + 4096, 4096, "p (k t) -> p k t", k=KD)

        u_r = region(0, 1024, "p (j t) -> p j t", j=4)
        u_k = region(1024, 2048, "p (j t) -> p j t", j=4)
        u_v = region(3072, 2048, "p (j t) -> p j t", j=4)
        u_w, u_a, u_g = region(5120, 512), region(5632, 512), region(6144, 256)
        LW = region(6400, 4096, "p (x t) -> p x t", x=8)
        AG = region(10496, 4096, "p (x t) -> p x t", x=8)
        ARL = region(14592, 4096, "p (x c n) -> p x c n", x=8, c=4)
        ARC = region(18688, 2048, "p (x c n) -> p x c n", x=8, c=4)
        KK = region(20736, 2048, "p (j t) -> p j t", j=4)
        TMP = 22784
        cumt, e1, e2, e3, e4 = (region(TMP + 512 * i, 512) for i in range(5))
        dch = small[:, 0:64].rearrange("p (x c) -> p x c", x=8)
        g_out = A[:, 0:4, 0:CTX]
        SC = {}
        for d, spans in enumerate((((1024, 2048), (5120, 1280)), ((20736, 2048), (22784, 2560)))):
            o, o2 = spans[0][0], spans[1][0]
            SC[d] = dict(
                BM=region(o, 512, "p (j n) -> p j n", j=4), KM=region(o + 512, 512, "p (j n) -> p j n", j=4),
                MA=region(o + 1024, 512, "p (j n) -> p j n", j=4),
                Ad=region(o + 1536, 256, "p (j n) -> p j n", j=4), Ao=region(o + 1792, 256, "p (j n) -> p j n", j=4),
                bt=region(o2, 256, "p (j n) -> p j n", j=4), kt=region(o2 + 256, 256, "p (j n) -> p j n", j=4),
                vt=region(o2 + 512, 256, "p (j n) -> p j n", j=4), Pt=region(o2 + 768, 256, "p (j n) -> p j n", j=4),
                X=region(o2 + 1024, 256, "p (j n) -> p j n", j=4))
            SC[d]["Uu"] = SC[d]["MA"][:, :, 0:64]
            SC[d]["state"] = sw[:, 1024 + 256 * d:1280 + 256 * d].rearrange("p (j n) -> p j n", j=4)
        ysum = sw[:, 0:1024].rearrange("p (c j n) -> p c j n", c=4, j=4)
        rk_t = u_r
        rwo = region(14592, 1024, "p (j t) -> p j t", j=4)
        ysq = region(15616, 1024, "p (x n) -> p x n", x=16)

        sig = region(0, 6 * 256, "p (x t) -> p x t", x=6)
        merged = region(1536, 2048, "p (k t) -> p k t", k=KD)
        sq_m = region(16640, 4096, "p (k t) -> p k t", k=KD)
        tok2 = region(0, 2048, "p (i n) -> p i n", i=2)
        yacc = region(2048, 2048, "p (i n) -> p i n", i=2)
        logit = region(4096, 72, "p (i n) -> p i n", i=2)
        msk = region(4168, 64, "p (i n) -> p i n", i=2)
        gat = region(4232, 64, "p (i n) -> p i n", i=2)
        posm = region(4296, 64, "p (i n) -> p i n", i=2)
        r8 = region(4360, 256)
        sel = region(4736, 2 * PAIR, "p (i n) -> p i n", i=2)
        selg = region(4992, 2 * PAIR, "p (i n) -> p i n", i=2)
        hte = region(5248, KD * PAIR)
        sgl, actv = region(6272, 512), region(7296, 512)
        actT = region(8320, 4 * PAIR)
        pgt = region(8832, SEQ)
        yex = region(9344, D)

        picked = region(11400, 2 * (ITEMS + 2), "p (i n) -> p i n", i=2)
        weight = region(11500, 2 * (ITEMS + 2), "p (i n) -> p i n", i=2)
        in_item = region(12200, ITEMS)
        slotT, gateT = region(11600, SEQ), region(11856, SEQ)
        lcol = region(12112, 8)
        item64 = region(12120, ITEMS)

        ql = region(0, 4096, "p (h t) -> p h t", h=8)
        qr = region(4096, 1024, "p (x t) -> p x t", x=2)
        kr = region(5120, 2048, "p (x t) -> p x t", x=4)
        ckv = region(7168, 512)
        mv = region(7680, 2048, "p (i n) -> p i n", i=4)
        naq = region(9728, 2048, "p (j t) -> p j t", j=4)
        nak = region(11776, 2048, "p (j t) -> p j t", j=4)
        nav = region(13824, 2048, "p (i n) -> p i n", i=4)
        nab = region(15872, 4096, "p (h x) -> p h x", h=8)
        ATT2 = 19968
        pq = region(ATT2, 1024, "p (x t) -> p x t", x=2)
        krt = region(ATT2 + 1024, 512)
        nope = A[:, 0:4, :]
        osb = A
        sq_b = region(14336, 4096, "p (k t) -> p k t", k=KD)
        xtok2 = region(20480, 2048, "p (i n) -> p i n", i=2)
        hid = region(0, FT * T, "p (f t) -> p f t", f=FT)
        sgf = region(FT * T, 1024, "p (x t) -> p x t", x=2)
        oq = region(0, 2048, "p (j t) -> p j t", j=8)
        okk = region(2048, 512)
        ov = region(2560, 512, "p (i n) -> p i n", i=4)
        oo = region(3072, 2048, "p (j t) -> p j t", j=8)
        res = region(18432, 2048, "p (i n) -> p i n", i=2)

        qk_sq = region(ATT + 3072, 1024, "p (x t) -> p x t", x=2)
        rs2 = region(ATT, 1024, "p (x t) -> p x t", x=2)
        pads = [region(ATT + 1024 + 288 * x, 288) for x in range(4)]
        dstd = region(ATT + 5120, 1024, "p (h t) -> p h t", h=4)
        RKs = region(5120, 1024, "p (j t) -> p j t", j=4)
        bon = region(16640, 256)
        rtmp = region(ATT2, 256)
        cnt_c, swa_c = region(16640, 1024), region(5120, 512)

        def ktvt(d):
            o = 5120 if d == 0 else 22784
            return region(o + 256, 512)

        marks = {}

        def work(base):
            b = lambda o, n: [region(base + 512 * (o + i), 512) for i in range(n)]
            return b(0, 3), b(3, 4), b(7, 3)

        def item(t, base, qk, nk, scale, rows, pv, to, bias=None, sink=None, comb=None):
            s, p, tr = work(base)
            return dict(qk=qk, nk=nk, scale=scale, rows=rows, pv=pv, out=to, bias=bias, sink=sink, comb=comb,
                        s=s[t % 3], p=p[t % 4], before=p[(t - 1) % 4], t=tr[t % 3])

        def diff_items():
            out = []
            for h in range(4):
                for qt in range(2):
                    for m in range(2):
                        r = slice(64 * m, 64 * m + 64)
                        qs = slice(qt * P, (qt + 1) * P)
                        pv = (lambda x, h=h: v_in[:, x, h * P:(h + 1) * P]) if m else None
                        out.append(item(len(out), ATT, [(q_in[r, h, qs], k_in[r, h, :])], T, 64 ** -0.5, (0, P), pv,
                                        w1a[:, h, qs], comb="second" if m else "first"))
            return out

        def mla_items():
            out = []
            for h in range(8):
                for i in range(4):
                    nk = T if i >= 2 else CTX
                    qs, r = slice(i * P, (i + 1) * P), (64 * (h % 2), 64 * (h % 2) + 64)
                    out.append(item(len(out), ATT2, [(ql[:, h, qs], ckv[:, 0:nk]), (qr[:, h // 4, qs], kr[:, h % 4, 0:nk])],
                                    nk, 96 ** -0.5, r, lambda x, h=h: mv[:, x, h * 64:(h + 1) * 64],
                                    osb[r[0]:r[1], h // 2, qs]))
            return out

        def na_items():
            out = []
            for h in range(8):
                for i in range(4):
                    nk = T if i >= 2 else CTX
                    qs, r = slice(i * P, (i + 1) * P), (64 * (h % 2), 64 * (h % 2) + 64)
                    out.append(item(len(out), ATT2, [(naq[r[0]:r[1], h // 2, qs], nak[r[0]:r[1], h // 2, 0:nk])],
                                    nk, 64 ** -0.5, r, lambda x, h=h: nav[:, x, h * 64:(h + 1) * 64],
                                    osb[r[0]:r[1], 4 + h // 2, qs],
                                    bias=nab[:, h, (i - 2) * SEQ:(i - 1) * SEQ] if i >= 2 else None))
            return out

        def swa_items():
            out = []
            for h in range(16):
                for qt in range(2):
                    r, kv = (64 * (h // 8), 64 * (h // 8) + 64), h // 8
                    qs = slice(qt * P, (qt + 1) * P)
                    out.append(item(len(out), ATT2, [(oq[r[0]:r[1], h % 8, qs], okk[r[0]:r[1], :])],
                                    T, 64 ** -0.5, r, lambda x, kv=kv: ov[:, x, kv * 64:(kv + 1) * 64],
                                    oo[r[0]:r[1], h % 8, qs], bias=swa_c[:, qt * SEQ:(qt + 1) * SEQ],
                                    sink=Q("sinks", h)))
            return out

        block = ctx.enter_context(nc.Block())

        def barrier(side, name, k):
            me = side if isinstance(side, str) else side.name
            eng = {"pe": nc.tensor, "act": nc.scalar, "dve": nc.vector}[me]
            if me != "pe":
                if side.n_back:
                    eng.wait_ge(side.back, side.n_back)
                if side.n_chain:
                    eng.wait_ge(side.chain, side.n_chain)
            eng.nop().then_inc(S(f"{me}_at_phase"), 1)
            for other in ("pe", "act", "dve"):
                if other != me:
                    eng.wait_ge(S(f"{other}_at_phase"), k)

        @block.tensor
        def _(pe):
            st = {"n": 0, "rr": 0, "unit": 0, "loop": None, "banks": 8}
            gave = {"act": 0, "dve": 0}
            last_user = [None] * 8
            tpos = {"base": 0}

            def at(key, v):
                if st["loop"] is None:
                    return v
                it, step = st["loop"]
                return v + it * step[key]

            def job(reader, own=False):
                b = 7 if own else st["rr"] % st["banks"]
                st["rr"] += not own
                if last_user[b] is not None:
                    who, n = last_user[b]
                    pe.wait_ge(back[who], at("back_" + who, n))
                return b, reader

            def done(j, last):
                b, reader = j
                last.then_inc(full, 1)
                st["n"] += 1
                gave[reader] += 1
                last_user[b] = (reader, gave[reader])
                reads[reader].append((banks[b], st["n"]))

            def drained(*who):
                for w in who or ("act", "dve"):
                    if gave[w]:
                        pe.wait_ge(back[w], at("back_" + w, gave[w]))

            def unit(n=1):
                u = st["unit"]
                t, o = divmod(u, UPT)
                assert o + n <= UPT
                if o == 0:
                    pe.wait_ge(ring_full[t % RING], at("tile", 16 * (t // RING + 1)))
                st["unit"] += n
                if o + n == UPT:
                    tile_free.append(st["n"] + 1)
                s = t % RING
                return ring[:, s * TILE + o * P:s * TILE + (o + n) * P]

            def mm(o, l, r, start, stop, **kw):
                return nc.tensor.matmul(o, l, r, start=start, stop=stop, **kw)

            def phase(k):
                if st["n"]:
                    pe.wait_ge(full, st["n"])
                barrier("pe", "", k)

            def modulation(x, of, cond):
                if x and x % KD == 0:
                    pe.wait_ge(back["act"], st["rows"])
                    j = job("dve")
                    for c in range(4):
                        last = nc.tensor.transpose(banks[j[0]][:, c * P:(c + 1) * P], rs_t[:, c * P:(c + 1) * P], ident)
                    done(j, last)
                if x == of:
                    return
                k = x % KD
                if k == 0:
                    st["mod"] = job("act", own=True)
                b = banks[st["mod"][0]]
                ws = unit(UPT)
                for g in range(4):
                    last = mm(b[32 * g:32 * g + 32, :], cond[:, k, :], ws[:, g * 512:(g + 1) * 512],
                              k == 0, k == KD - 1)
                if k < KD - 1:
                    last.then_inc(full, 1)
                    st["n"] += 1
                else:
                    done(st["mod"], last)
                    st["rows"] = gave["act"]

            def transposes_in(src, cols, name):
                marks[name] = dict(gave)
                pe.wait_ge(S(name), 16)
                n = src.shape[1]
                for k in range(KD):
                    j = job("act")
                    for i in range(n):
                        last = nc.tensor.transpose(banks[j[0]][:, i * P:(i + 1) * P], src[:, i, k * P:(k + 1) * P], ident)
                    done(j, last)

            def norm(name, sq, cols):
                marks[name] = dict(gave)
                n = cols.stop - cols.start
                j = job("act")
                for k in range(KD):
                    pe.wait_ge(S("squared_" + name), k + 1)
                    last = mm(banks[j[0]][:, 0:n], ones, sq[:, k, 0:n], k == 0, k == KD - 1)
                done(j, last)

            def project(m_tiles, cols, reader, src=A, kt=KD, name=None):
                n = cols.stop - cols.start
                for m in range(m_tiles):
                    j = job(reader)
                    for k in range(kt):
                        last = mm(banks[j[0]][:, 0:n], unit(), src[:, k, cols], k == 0, k == kt - 1)
                    done(j, last)

            def project_tok(reader, src=A):
                w = [unit(4) for _ in range(KD)]
                tile_free[-2] = tile_free[-1] = st["n"] + 4
                for i in range(4):
                    j = job(reader)
                    for k in range(KD):
                        last = mm(banks[j[0]][:, :], src[:, k, i * P:(i + 1) * P], w[k], k == 0, k == KD - 1)
                    done(j, last)

            def attention(name, items):
                n = len(items)
                turned = {}
                for t in range(n + 4):
                    if t < n:
                        it = items[t]
                        if "need" in it:
                            for who in it["need"]:
                                pe.wait_ge(S(who[0]), who[1])
                        j = job("dve")
                        for x, (l, r) in enumerate(it["qk"]):
                            last = mm(banks[j[0]][:, 0:it["nk"]], l, r, x == 0, x == len(it["qk"]) - 1)
                        done(j, last)
                    if 0 <= t - 2 < n and items[t - 2]["pv"] is not None:
                        it = items[t - 2]
                        pe.wait_ge(S("prob_" + name), t - 1)
                        j = job("act")
                        for x in range(it["nk"] // P):
                            last = nc.tensor.transpose(banks[j[0]][:, x * P:(x + 1) * P],
                                                       it["p"][:, x * P:(x + 1) * P], ident)
                        done(j, last)
                        turned[t - 2] = gave["act"]
                    if 0 <= t - 4 < n and items[t - 4]["pv"] is not None:
                        it = items[t - 4]
                        pe.wait_ge(back["act"], turned[t - 4])
                        j = job("dve")
                        lo, hi = it["rows"]
                        nk = it["nk"] // P
                        for x in range(nk):
                            last = mm(banks[j[0]][lo:hi, 0:P], it["pv"](x), it["t"][:, x * P:(x + 1) * P],
                                      x == 0, x == nk - 1)
                        done(j, last)

            def out_proj(src, n, name):
                marks[name] = dict(gave)
                for m in range(KD):
                    j = job("dve")
                    for k in range(KD):
                        last = mm(banks[j[0]][:, 0:n], unit(), src(k), k == 0, k == KD - 1)
                    done(j, last)

            def ffn(n, name):
                marks[name] = dict(gave)
                for f in range(FT):
                    for reader in ("act", "dve"):
                        j = job(reader)
                        for k in range(KD):
                            last = mm(banks[j[0]][:, 0:n], unit(), A[:, k, T - n:T], k == 0, k == KD - 1)
                        done(j, last)
                drained("dve")
                marks["res_" + name] = dict(gave)
                for m in range(KD):
                    j = job("dve")
                    for f in range(FT):
                        last = mm(banks[j[0]][:, 0:n], unit(), hid[:, f, 0:n], f == 0, f == FT - 1)
                    done(j, last)

            pe.wait_ge(S("params_in"), 32)
            pe.wait_ge(S("small_in"), 16)
            transposes_in(xtok, None, "x_in")
            norm("n1", sq_t, slice(0, T))
            pe.wait_ge(S("silu_c"), 1)
            st["banks"] = 7
            for x in range(ADA + 1):
                modulation(x, ADA, cond1)
            st["banks"] = 8
            pe.wait_ge(S("normed_n1"), KD)
            marks["proj1"] = dict(gave)
            project(4, LAT, "act")
            project(4, LAT, "act")
            project(4, slice(0, T), "act")
            project_tok("act")
            for g in range(4):
                pe.wait_ge(S("pool_diff"), g + 1)
                j = job("dve")
                last = mm(banks[j[0]][:, 0:SEQ], sw1["pool_w"][:, g * P:(g + 1) * P], w1a[:, g, :], True, True)
                done(j, last)
            marks["qk"] = dict(gave)
            for x in range(8):
                n = SEQ if x < 4 else T
                pe.wait_ge(S("qk_sq"), x + 1)
                j = job("act")
                last = mm(banks[j[0]][:, 0:n], blk, qk_sq[:, x % 2, 0:n], True, True)
                done(j, last)
                pe.wait_ge(S("qk_normed"), x + 1)
                src = q_in[:, x, :] if x < 4 else k_in[:, x - 4, LAT]
                j = job("dve")
                last = mm(banks[j[0]][:, 0:SEQ], C("perm64"), src, True, True)
                done(j, last)
            pe.wait_ge(S("rotated"), 8)
            attention("diff", diff_items())
            marks["diffnorm"] = dict(gave)
            for h in range(4):
                pe.wait_ge(S("diff_sq"), h + 1)
                j = job("act")
                last = mm(banks[j[0]][:, 0:SEQ], ones, w1b[:, h, :], True, True)
                done(j, last)
            phase(1)
            project(4, LAT, "dve")
            project(11, slice(0, T), "dve")
            for k in range(KD):
                unit()
            tile_free[-1] = st["n"]
            drained("dve")
            pe.wait_ge(S("lora_in"), 2)
            marks["lora"] = dict(gave)
            for x in range(8):
                d, jt = divmod(x, 4)
                for wname, src in (("w2", u_w), ("a2", u_a)):
                    j = job("act")
                    last = mm(banks[j[0]][:, :], sw1[wname][64 * d:64 * d + 64, jt * P:(jt + 1) * P],
                              src[64 * d:64 * d + 64, :], True, True)
                    done(j, last)
            for jt in range(4):
                j = job("act")
                last = mm(banks[j[0]][:, 0:SEQ], sw1["g2"][:, jt * P:(jt + 1) * P], u_g, True, True)
                done(j, last)
            for jt in range(4):
                pe.wait_ge(S("kk_sq"), jt + 1)
                j = job("act")
                last = mm(banks[j[0]][:, :], blk, e1 if jt % 2 == 0 else e2, True, True)
                done(j, last)
            phase(2)

            def quad(o, l, r, start=True, stop=True):
                for hh in range(2):
                    h = slice(64 * hh, 64 * hh + 64)
                    last = mm(o[h], l[h], r[h], start, stop)
                return last

            later = iter(range(2 * ADA + 1))
            modulate_later = lambda: modulation(next(later), 2 * ADA, cond2)
            st["banks"] = 7
            pe.wait_ge(S("silu_c"), 2)
            for step in range(NCH):
                lat = step >= NCH // 2
                cs = [step, (3 - step) if not lat else (NCH - 1 - (step - 4))]
                two = 128 if lat else 64

                def ar(d, jt, c):
                    x = 4 * d + jt
                    return ARL[:, x, c - 4, :] if lat else ARC[:, x, c, :]

                tk = lambda c: slice(c * CH, (c + 1) * CH)
                ready = {}
                marks["step", step] = dict(gave)
                for d in range(2):
                    c = cs[d]
                    for src in (AG, LW):
                        j = job("dve")
                        b = banks[j[0]][:, :].rearrange("p (j n) -> p j n", j=4)
                        for jt in range(4):
                            last = quad(b[:, jt, 0:two], src[:, 4 * d + jt, tk(c)], ar(d, jt, c))
                        done(j, last)
                    j = job("dve")
                    b = banks[j[0]][:, :].rearrange("p (x j n) -> p x j n", x=2, j=4)
                    for jt in range(4):
                        quad(b[:, 0, jt, :], ar(d, jt, c)[:, 0:64], AG[:, 4 * d + jt, tk(c)])
                        last = quad(b[:, 1, jt, :], AG[:, 4 * d + jt, tk(c)], id2)
                    done(j, last)
                    j = job("act")
                    b = banks[j[0]][:, :].rearrange("p (x j n) -> p x j n", x=2, j=4)
                    for jt in range(4):
                        quad(b[:, 0, jt, :], LW[:, 4 * d + jt, tk(c)], id2)
                        last = quad(b[:, 1, jt, :], u_v[:, jt, tk(c)], id2)
                    done(j, last)
                    ready[d] = dict(gave)
                modulate_later()
                for level in range(5):
                    for d in range(2):
                        w = SC[d]
                        for who in ready[d]:
                            pe.wait_ge(back[who], ready[d][who])
                        if level > 0:
                            j = job("dve")
                            b = banks[j[0]][:, 0:256].rearrange("p (j n) -> p j n", j=4)
                            for jt in range(4):
                                last = quad(b[:, jt, :], w["MA"][:, jt, 64:128], w["Pt"][:, jt, :])
                            done(j, last)
                        if level < 4:
                            j = job("act")
                            b = banks[j[0]][:, :].rearrange("p (j n) -> p j n", j=4)
                            for jt in range(4):
                                mk = w["BM"][:, jt, 0:64] if level == 0 else w["MA"][:, jt, 0:64]
                                ak = w["Ad"][:, jt, :] if level == 0 else w["MA"][:, jt, 64:128]
                                if level < 3:
                                    quad(b[:, jt, 0:64], ak, mk)
                                last = quad(b[:, jt, 64:128], mk, ak)
                            done(j, last)
                        ready[d] = dict(gave)
                    if level:
                        modulate_later()
                for d in range(2):
                    w = SC[d]
                    pe.wait_ge(back["dve"], ready[d]["dve"])
                    j = job("act")
                    b = banks[j[0]][:, :].rearrange("p (j n) -> p j n", j=4)
                    for jt in range(4):
                        quad(b[:, jt, 0:64], w["Ao"][:, jt, :], w["Pt"][:, jt, :])
                        last = quad(b[:, jt, 64:128], w["Pt"][:, jt, :], id2)
                    done(j, last)
                    ready[d] = dict(gave)
                for d in range(2):
                    w = SC[d]
                    pe.wait_ge(back["act"], ready[d]["act"])
                    j = job("dve")
                    b = banks[j[0]][:, 0:256].rearrange("p (j n) -> p j n", j=4)
                    for jt in range(4):
                        last = quad(b[:, jt, :], w["MA"][:, jt, 64:128], w["MA"][:, jt, 0:64])
                    done(j, last)
                    ready[d] = dict(gave)
                modulate_later()
                ready_x, ready_u = {}, {}
                for d in range(2):
                    w, c = SC[d], cs[d]
                    if step:
                        pe.wait_ge(S("state_ready"), 2 * (step - 1) + d + 1)
                    j = job("act")
                    b = banks[j[0]][:, 0:256].rearrange("p (j n) -> p j n", j=4)
                    for jt in range(4):
                        for hh in range(2):
                            h = slice(64 * hh, 64 * hh + 64)
                            if step:
                                mm(b[h, jt, :], ar(d, jt, c)[h, 0:64], w["state"][h, jt, :], True, False)
                            last = mm(b[h, jt, :], w["KM"][h, jt, 0:64], w["vt"][h, jt, :], not step, True)
                    done(j, last)
                    ready_x[d] = gave["act"]
                for d in range(2):
                    w = SC[d]
                    pe.wait_ge(back["act"], ready_x[d])
                    pe.wait_ge(back["dve"], ready[d]["dve"])
                    j = job("act")
                    b = banks[j[0]][:, 0:256].rearrange("p (j n) -> p j n", j=4)
                    for jt in range(4):
                        last = quad(b[:, jt, :], w["Pt"][:, jt, :], w["X"][:, jt, :])
                    done(j, last)
                    ready_u[d] = gave["act"]
                for d in range(2):
                    w, c = SC[d], cs[d]
                    pe.wait_ge(back["act"], ready_u[d])
                    if lat:
                        j = job("dve")
                        b = banks[j[0]][:, 0:256].rearrange("p (j n) -> p j n", j=4)
                        for jt in range(4):
                            for hh in range(2):
                                h = slice(64 * hh, 64 * hh + 64)
                                mm(b[h, jt, :], ar(d, jt, c)[h, 64:128], w["state"][h, jt, :], True, False)
                                mm(b[h, jt, :], w["BM"][h, jt, 64:128], w["Uu"][h, jt, :], False, False)
                                last = mm(b[h, jt, :], w["KM"][h, jt, 64:128], w["vt"][h, jt, :], False, True)
                        done(j, last)
                    if step < NCH - 1:
                        j = job("dve")
                        b = banks[j[0]][:, 0:256].rearrange("p (j n) -> p j n", j=4)
                        for jt in range(4):
                            for hh in range(2):
                                h = slice(64 * hh, 64 * hh + 64)
                                mm(b[h, jt, :], w["bt"][h, jt, :], w["Uu"][h, jt, :], True, False)
                                last = mm(b[h, jt, :], w["kt"][h, jt, :], w["vt"][h, jt, :], False, True)
                        done(j, last)
            modulate_later()
            st["banks"] = 8
            pe.wait_ge(S("y_normed"), 1)
            for half in range(2):
                j = job("dve")
                b = banks[j[0]][:, :].rearrange("p (j c n) -> p j c n", j=2, c=4)
                for j2 in range(2):
                    for c in range(4):
                        last = quad(b[:, j2, c, :], ysum[:, c, 2 * half + j2, :], id2)
                done(j, last)
            for jt in range(4):
                j = job("dve")
                last = mm(banks[j[0]][:, 0:SEQ], blk, rk_t[:, jt, :], True, True)
                done(j, last)
            phase(3)
            marks["merge"] = dict(gave)
            branch = [lambda k: pool_out[:, k, :], lambda k: att_out[:, k, :], lambda k: rwo[:, k, :]]
            for m in range(KD):
                for n in range(3):
                    j = job("act")
                    for k in range(KD):
                        last = mm(banks[j[0]][:, 0:SEQ], unit(), A[:, k, LAT], k == 0, k == KD - 1)
                    done(j, last)
                    j = job("dve")
                    for k in range(JT):
                        last = mm(banks[j[0]][:, 0:SEQ], unit(), branch[n](k), k == 0, k == JT - 1)
                    done(j, last)
            pe.wait_ge(S("branch_mixed"), 3 * KD)
            out_proj(lambda k: merged[:, k, :], SEQ, "res_n2")
            norm("n2", sq_m, LAT)
            pe.wait_ge(S("normed_n2"), KD)
            phase(4)
            for i in range(2):
                j = job("dve")
                for k in range(KD):
                    last = mm(banks[j[0]][:, 0:36], A[:, k, CTX + i * P:CTX + (i + 1) * P],
                              sw1["router"][:, k * 36:(k + 1) * 36], k == 0, k == KD - 1)
                done(j, last)
            for i in range(2):
                for half in range(2):
                    j = job("act")
                    for k in range(4):
                        last = nc.tensor.transpose(banks[j[0]][:, k * P:(k + 1) * P],
                                                   A[:, 4 * half + k, CTX + i * P:CTX + (i + 1) * P], ident)
                    done(j, last)
            pe.wait_ge(S("routed"), 1)
            j = job("dve")
            b = banks[j[0]]
            mm(b[:, 0:32], C("tri"), msk[:, 0, :], True, True)
            mm(b[:, 32:64], ones, msk[:, 0, :], True, False)
            mm(b[:, 32:64], C("tri"), msk[:, 1, :], False, True)
            mm(b[0:NE, 64:65], msk[:, 0, :], ones[:, 0:1], True, False)
            last = mm(b[0:NE, 64:65], msk[:, 1, :], ones[:, 0:1], False, True)
            done(j, last)
            pe.wait_ge(S("counted"), 1)
            j = job("dve")
            b = banks[j[0]]
            last = mm(b[0:NE, 0:1], C("tri")[0:NE, 0:NE], lcol[0:NE, 1:2], True, True)
            done(j, last)
            j = job("dve")
            b = banks[j[0]]
            for i in range(2):
                nc.tensor.transpose(b[0:NE, i * P:(i + 1) * P], posm[:, i, :], ident)
                last = nc.tensor.transpose(b[0:NE, SEQ + i * P:SEQ + (i + 1) * P], gat[:, i, :], ident)
            done(j, last)
            drained("dve")
            pe.wait_ge(S("items_cut"), 1)
            j = job("dve")
            b = banks[j[0]]
            for i in range(2):
                mm(b[:, i * ITEMS:(i + 1) * ITEMS], slotT[0:NE, i * P:(i + 1) * P], in_item[0:NE, :], True, True)
                mm(b[:, (2 + i) * ITEMS:(3 + i) * ITEMS], gateT[0:NE, i * P:(i + 1) * P], in_item[0:NE, :], True, True)
            last = mm(b[0:1, 4 * ITEMS:5 * ITEMS], C("number")[0:NE, :], in_item[0:NE, :], True, True)
            done(j, last)
            phase(5)
            n0, g0, u0, f0 = st["n"], dict(gave), st["unit"], len(tile_free)
            order = ("act", "act", "dve", "act", "dve", "act", "act", "dve") + ("dve",) * 4
            per = {"n": len(order), "act": order.count("act"), "dve": order.count("dve")}
            drained()
            last_user[:] = [None] * 8
            for x, who in enumerate(order):
                last_user[x % 8] = (who, gave[who] - per[who] + order[:x + 1].count(who))
            with nc.tensor.Fori(0, ITEMS // 2) as it:
                st["loop"] = (it, {"back_act": per["act"], "back_dve": per["dve"],
                                   "tile": 16 * BODY // RING})
                st["rr"] = 0
                pe.wait_ge(S("selected"), it + 1)
                for half in range(2):
                    j = job("act")
                    for k in range(4):
                        for i in range(2):
                            c = (4 * half + k) * P
                            last = mm(banks[j[0]][:, k * PAIR:(k + 1) * PAIR], tok2[:, i, c:c + P], sel[:, i, :],
                                      i == 0, i == 1)
                    done(j, last)
                j = job("dve")
                for i in range(2):
                    last = mm(banks[j[0]][:, i * P:(i + 1) * P], selg[:, i, :], ident, True, True)
                done(j, last)
                pe.wait_ge(back["act"], at("back_act", gave["act"]))

                def two_experts(reader, src, tiles):
                    j = job(reader)
                    for t in range(tiles):
                        ws = [[unit(4) for _ in range(4)] for x in range(2)]
                        for k in range(4):
                            for x in range(2):
                                c = (4 * t + k) * PAIR + SLOTS * x
                                last = mm(banks[j[0]][SLOTS * x:SLOTS * (x + 1), :], src[:, c:c + SLOTS], ws[x][k],
                                          t + k == 0, 4 * t + k == 4 * tiles - 1)
                    if tiles == 2:
                        tile_free[-4] = tile_free[-3] = st["n"] + 1
                    done(j, last)

                marks["expert"] = dict(gave)
                two_experts("act", hte, 2)
                two_experts("dve", hte, 2)
                pe.wait_ge(back["dve"], at("back_dve", gave["dve"]))
                j = job("act")
                for c in range(4):
                    last = nc.tensor.transpose(banks[j[0]][:, c * PAIR:(c + 1) * PAIR], actv[:, c * P:(c + 1) * P], ident)
                done(j, last)
                pe.wait_ge(back["act"], at("back_act", gave["act"]))
                two_experts("act", actT, 1)
                two_experts("dve", actT, 1)
                drained()
                for i in range(2):
                    for half in range(2):
                        j = job("dve")
                        last = mm(banks[j[0]][:, :], pgt[:, i * P:(i + 1) * P], yex[:, half * 512:(half + 1) * 512],
                                  True, True)
                        done(j, last)
            st["loop"] = None
            assert st["n"] - n0 == per["n"], (st["n"] - n0, per)
            assert all(gave[w] - g0[w] == per[w] for w in gave), (gave, g0, per)
            assert st["unit"] - u0 == BODY * UPT and len(tile_free) - f0 == BODY
            marks["moe"] = dict(n0=n0, f0=f0, per=dict(per), act0=g0["act"], dve0=g0["dve"])
            rest = ITEMS // 2 - 1
            st["n"] += rest * per["n"]
            for w in gave:
                gave[w] += rest * per[w]
            st["unit"] += rest * BODY * UPT
            body = tile_free[f0:]
            for r in range(1, rest + 1):
                tile_free.extend(v + r * per["n"] for v in body)
            last_user[:] = [None] * 8
            drained()
            for k2 in range(4):
                j = job("dve")
                for kk_ in range(2):
                    for i in range(2):
                        o = (2 * kk_ + i) * P
                        k = 2 * k2 + kk_
                        last = nc.tensor.transpose(banks[j[0]][:, o:o + P], yacc[:, i, k * P:(k + 1) * P], ident)
                done(j, last)
            phase(6)

            transposes_in(xtok2, None, "x2_in")
            norm("n3", sq_b, slice(0, T))
            pe.wait_ge(S("normed_n3"), KD)
            marks["proj2"] = dict(gave)
            project(4, slice(0, T), "dve")
            project(8, slice(0, T), "act")
            project_tok("act")
            phase(7)
            pe.wait_ge(S("small_in"), 32)
            marks["mla"] = dict(gave)
            pe.wait_ge(S("mla_sq"), 2)
            j = job("act")
            mm(banks[j[0]][:, :], ones, osb[:, 4, :], True, False)
            last = mm(banks[j[0]][:, :], ones, osb[:, 5, :], False, True)
            done(j, last)
            pe.wait_ge(S("mla_sq"), 3)
            j = job("act")
            last = mm(banks[j[0]][:, :], ones, osb[:, 6, :], True, True)
            done(j, last)
            pe.wait_ge(S("mla_normed"), 3)
            for m in range(6):
                j = job("dve")
                for k in range(2):
                    last = mm(banks[j[0]][:, :], sw2["q_up"][:, k * 768 + m * P:k * 768 + (m + 1) * P],
                              pq[:, k, :], k == 0, k == 1)
                done(j, last)
            drained("dve")
            for x in range(3):
                src = krt[:, LAT] if x == 2 else qr[:, x, LAT]
                j = job("dve")
                last = mm(banks[j[0]][:, 0:SEQ], C("perm32"), src, True, True)
                done(j, last)
            marks["uk"] = dict(gave)
            for h in range(8):
                p0 = 64 * (h % 2)
                j = job("act")
                last = mm(banks[j[0]][:, :], sw2["uk"][p0:p0 + 64, (h // 2) * P:(h // 2 + 1) * P],
                          nope[p0:p0 + 64, h // 2, :], True, True)
                done(j, last)
            for i in range(4):
                j = job("act")
                last = mm(banks[j[0]][:, :], ckv[:, i * P:(i + 1) * P], sw2["uv"], True, True)
                done(j, last)
            drained()
            pe.wait_ge(S("kr_banded"), 4)
            phase(8)
            attention("mla", mla_items())
            phase(9)
            attention("na", na_items())
            phase(10)
            out_proj(lambda k: osb[:, k, :], T, "res_n4")
            norm("n4", sq_b, slice(0, T))
            pe.wait_ge(S("normed_n4"), KD)
            phase(11)
            ffn(T, "f0")
            phase(12)
            norm("n5", sq_b, slice(0, T))
            pe.wait_ge(S("normed_n5"), KD)
            marks["proj3"] = dict(gave)
            project(8, LAT, "act")
            project(1, slice(0, T), "act")
            w = unit(8)
            tile_free[-1] = st["n"] + 1
            j = job("act")
            for i in range(4):
                for k in range(KD):
                    last = mm(banks[j[0]][:, i * P:(i + 1) * P], A[:, k, i * P:(i + 1) * P],
                              w[:, k * P:(k + 1) * P], k == 0, k == KD - 1)
            done(j, last)
            drained()
            for x in range(9):
                src = okk[:, LAT] if x == 8 else oq[:, x, :]
                j = job("dve")
                last = mm(banks[j[0]][:, 0:SEQ], C("perm64"), src, True, True)
                done(j, last)
            drained()
            phase(13)
            attention("swa", swa_items())
            drained()
            out_proj(lambda k: oo[:, k, :], SEQ, "res_n6")
            norm("n6", sq_b, LAT)
            pe.wait_ge(S("normed_n6"), KD)
            phase(14)
            ffn(SEQ, "f1")
            norm("n7", sq_b, LAT)
            pe.wait_ge(S("normed_n7"), KD)
            for i in range(2):
                for half in range(2):
                    j = job("act")
                    for k in range(4):
                        last = nc.tensor.transpose(banks[j[0]][:, k * P:(k + 1) * P],
                                                   A[:, 4 * half + k, CTX + i * P:CTX + (i + 1) * P], ident)
                    done(j, last)
            assert st["unit"] == N_TILES * UPT, (st["unit"] / UPT, N_TILES)

        @block.scalar
        def _(act):
            a = act_s
            f = nc.scalar.activation
            act.dma_start(par[:, :], dram["par"]).then_inc(S("params_in"), 16)
            act.dma_start(con[:, :], dram["con"]).then_inc(S("params_in"), 16)
            act.dma_start(arena[:, ATT:ATT + 4096], dram["xin"]).then_inc(S("x_in"), 16)
            act.dma_start(sw[:, 0:SW1_W], dram["sw1"]).then_inc(S("small_in"), 16)
            act.dma_start(region(16640, 1280), dram["cnt"]).then_inc(S("counts_in"), 16)
            act.wait_ge(S("params_in"), 32)

            def norm(name, sq, cols, after=None, lead=0):
                n = cols.stop - cols.start
                for k in range(KD):
                    if after:
                        act.wait_ge(back["dve"], marks[after]["dve"] + k + 1)
                    a.signals(f(sq[:, k, 0:n], H[:, k, cols], ACT.Square), "squared_" + name)
                b = a.take()
                a.gives(f(rs_t[:, 0:n], b[:, 0:n], ACT.Sqrt, bias=eps_c[:, 0:1], scale=1.0 / D))

            def modulate(name, cols, shift):
                for k in range(KD):
                    if name != "n1":
                        act.wait_ge(S("scaled_" + name), k + 1)
                    for x in ((0, 1) if cols.start == 0 else (0,)):
                        seg = LAT if x == 0 else slice(0, CTX)
                        sc = coef[:, 2 * k + x:2 * k + x + 1] if shift is not None else Q("final_norm", k)
                        bias = shift[:, 2 * k + x:2 * k + x + 1] if shift is not None else 0.0
                        ins = f(A[:, k, seg], A[:, k, seg], ACT.Identity, bias=bias, scale=sc)
                        if x == 1 or cols.start != 0:
                            a.signals(ins, "normed_" + name)

            def copies(n, dst):
                for x in range(n):
                    b = a.take()
                    o = dst(x)
                    a.given(f(o, view(b, o), ACT.Copy))

            def view(b, o):
                n = o.free_size()
                v = b[:, 0:n]
                if len(o.shape) == 3:
                    v = v.rearrange("p (a b) -> p a b", b=o.shape[2])
                return v

            def attention(name, items):
                n = len(items)
                for t in range(n + 4):
                    if t < n:
                        it = items[t]
                        act.wait_ge(S("max_" + name), t + 1)
                        cols = slice(MX + 4 * (t % 4), MX + 4 * (t % 4) + 4)
                        c = small[:, cols]
                        if it["sink"] is not None:
                            f(c[:, 2:3], it["sink"], ACT.Exp, bias=c[:, 0:1])
                        a.signals(f(it["p"][:, 0:it["nk"]], it["s"][:, 0:it["nk"]], ACT.Exp, bias=c[:, 0:1],
                                    accum_out=c[:, 1:2]), "exp_" + name)
                    if 0 <= t - 2 < n and items[t - 2]["pv"] is not None:
                        it = items[t - 2]
                        b = a.take()
                        a.given(f(it["t"][:, 0:it["nk"]], b[:, 0:it["nk"]], ACT.Copy))

            act.wait_ge(S("eps_set"), 1)
            c_of = lambda n: Q(n, 0, 16).rearrange("p (k x) -> p k x", x=2)
            a.signals(f(cond1[:, :, 0:2], c_of("c1"), ACT.Silu), "silu_c")

            def modulation(x):
                if x % KD == KD - 1:
                    b = a.take()
                    a.given(f(rs_t[:, :], b[:, :], ACT.Copy))

            copies(KD, lambda k: H[:, k, :])
            act.wait_ge(back["act"], a.n_back)
            norm("n1", sq_t, slice(0, T))
            act.wait_ge(S("root_used"), 1)
            for x in range(ADA):
                modulation(x)
            act.wait_ge(S("coef_n1"), 1)
            modulate("n1", slice(0, T), mod1[:, 0:16])
            copies(4, lambda j: pool_in[:, j, :])
            copies(4, lambda j: q_in[:, j, :])
            copies(4, lambda j: k_in[:, j, :])
            copies(4, lambda i: v_in[:, i, :])
            act.wait_ge(S("lam_dots"), 1)
            a.signals(f(small[:, LM + 2:LM + 4], small[:, LM:LM + 2], ACT.Exp), "lam_exp")
            for x in range(8):
                n = SEQ if x < 4 else T
                src = q_in[:, x, :] if x < 4 else k_in[:, x - 4, :]
                if x >= 2:
                    act.wait_ge(S("qk_normed"), x - 1)
                act.wait_ge(back["act"], marks["qk"]["act"])
                a.signals(f(qk_sq[:, x % 2, 0:n], src, ACT.Square), "qk_sq")
                b = a.take()
                a.gives(f(rs2[:, x % 2, 0:n], b[:, 0:n], ACT.Sqrt, bias=eps_c[:, 0:1], scale=1.0 / 64))
            attention("diff", diff_items())
            for h in range(4):
                act.wait_ge(S("diff_evac"), 1)
                a.signals(f(w1b[:, h, :], w1a[:, h, :], ACT.Square), "diff_sq")
                b = a.take()
                a.gives(f(dstd[:, h, :], b[:, 0:SEQ], ACT.Sqrt,
                          bias=eps_c[:, 0:1], scale=1.0 / P))
            barrier(a, "", 1)
            act.wait_ge(S("shifted"), 1)
            a.signals(f(u_w, u_w, ACT.Tanh), "lora_in")
            a.signals(f(u_g, u_g, ACT.Sigmoid), "lora_in")
            for x in range(8):
                for dst, bias in ((LW, "w0"), (AG, "a0")):
                    b = a.take()
                    a.given(f(dst[:, x, :], b[:, :], ACT.Sigmoid, bias=Q(bias, x)))
            for jt in range(4):
                b = a.take()
                a.given(f(g_out[:, jt, :], b[:, 0:SEQ], ACT.Copy))
            for jt in range(4):
                b = a.take()
                a.gives(f(e3 if jt % 2 == 0 else e4, b[:, :], ACT.Sqrt))
            for x in range(8):
                act.wait_ge(S("cumulated"), x + 1)
                f(dch[:, x, :], tots[:, x, :], ACT.Exp)
                f(e1, cumt, ACT.Exp)
                f(e2, e4, ACT.Exp)
                a.signals(f(e3, cumt, ACT.Exp, scale=-1.0), "exps")
            barrier(a, "", 2)
            act.wait_ge(S("cond_cleared"), 1)
            a.signals(f(cond2[:, :, 0:2], c_of("c2"), ACT.Silu), "silu_c")
            later = iter(range(2 * ADA))
            for step in range(NCH):
                for d in range(2):
                    b = a.take()
                    a.given(f(ktvt(d), b[:, :], ACT.Copy))
                modulation(next(later))
                for level in range(4):
                    for d in range(2):
                        b = a.take()[:, :].rearrange("p (j n) -> p j n", j=4)
                        lo = 0 if level < 3 else 64
                        a.given(f(SC[d]["MA"][:, :, lo:128], b[:, :, lo:128], ACT.Copy))
                    if level:
                        modulation(next(later))
                modulation(next(later))
                for d in range(2):
                    b = a.take()[:, :].rearrange("p (j n) -> p j n", j=4)
                    a.given(f(SC[d]["MA"], b, ACT.Copy))
                modulation(next(later))
                for key in ("X", "Uu"):
                    for d in range(2):
                        b = a.take()[:, 0:256].rearrange("p (j n) -> p j n", j=4)
                        a.given(f(SC[d][key], b, ACT.Copy))
            act.wait_ge(S("y_var"), 1)
            a.signals(f(small[:, GNC:GNC + 16], small[:, GNC:GNC + 16], ACT.Sqrt, bias=eps_c[:, 1:2], scale=1.0 / 64),
                      "y_std")
            barrier(a, "", 3)
            for i in range(3 * KD):
                if i >= 6:
                    act.wait_ge(S("branch_mixed"), i - 5)
                b = a.take()
                a.given(f(sig[:, i % 6, :], b[:, 0:SEQ], ACT.Sigmoid))
            norm("n2", sq_m, LAT, after="res_n2")
            modulate("n2", LAT, mod1[:, 48:64])
            barrier(a, "", 4)
            for i in range(2):
                for half in range(2):
                    b = a.take()
                    a.given(f(tok2[:, i, half * 512:(half + 1) * 512], b[:, :], ACT.Copy))
            for i in range(2):
                act.wait_ge(S("group_max"), i + 1)
                a.signals(f(r8[:, 100 + 8 * i:104 + 8 * i], logit[:, i, 0:4], ACT.Exp, bias=r8[:, 90 + i:91 + i],
                            accum_out=r8[:, 92 + i:93 + i]), "group_exp")
                act.wait_ge(S("top_two"), i + 1)
                a.signals(f(r8[:, 96 + i:97 + i], r8[:, 94 + i:95 + i], ACT.Exp), "top_exp")
            barrier(a, "", 5)
            m = marks["moe"]
            with nc.scalar.Fori(0, ITEMS // 2) as it:
                a.it, a.step = it, {"full": m["per"]["n"], "back_act": m["per"]["act"], "back_dve": m["per"]["dve"]}

                for half in range(2):
                    b = a.take()
                    a.given(f(hte[:, half * 512:(half + 1) * 512], b[:, :], ACT.Copy))
                b = a.take()
                a.given(f(sgl, b[:, :], ACT.Silu))
                b = a.take()
                a.given(f(actT, b[:, :], ACT.Copy))
                b = a.take()
                a.given(f(yex[:, 0:512], b[:, :], ACT.Copy))
            a.it = None
            a.n_back += (ITEMS // 2 - 1) * m["per"]["act"]
            barrier(a, "", 6)
            act.dma_start(sw[:, 0:SW2_W], dram["sw2"]).then_inc(S("small_in"), 16)
            act.dma_start(arena[:, 20480:22528], dram["xin2"]).then_inc(S("x2_in"), 16)
            copies(KD, lambda k: H[:, k, 0:CTX])
            act.wait_ge(back["act"], a.n_back)
            norm("n3", sq_b, slice(0, T))
            modulate("n3", slice(0, T), mod2a[:, 0:16])
            copies(4, lambda j: naq[:, j, :])
            copies(4, lambda j: nak[:, j, :])
            copies(4, lambda i: nav[:, i, :])
            barrier(a, "", 7)
            act.dma_start(arena[:, 15872:19968], dram["nab"]).then_inc(S("bias_in"), 16)
            for x in range(3):
                src = pq[:, x, :] if x < 2 else ckv
                a.signals(f(osb[:, 4 + x, :], src, ACT.Square), "mla_sq")
            for x in range(2):
                b = a.take()
                a.gives(f(osb[:, 4 + 3 * x, :] if x else rs_t[:, :], b[:, :], ACT.Sqrt, bias=eps_c[:, 0:1],
                          scale=1.0 / (256 if x == 0 else 128)))
            for h in range(8):
                b = a.take()
                a.given(f(ql[:, h, :], b[:, :], ACT.Copy))
            for i in range(4):
                b = a.take()
                a.given(f(mv[:, i, :], b[:, :], ACT.Copy))
            barrier(a, "", 8)
            attention("mla", mla_items())
            barrier(a, "", 9)
            attention("na", na_items())
            barrier(a, "", 10)
            norm("n4", sq_b, slice(0, T), after="res_n4")
            modulate("n4", slice(0, T), mod2a[:, 48:64])
            barrier(a, "", 11)

            def ffn(n, name):
                for g in range(FT):
                    if g >= 2:
                        act.wait_ge(back["dve"], marks[name]["dve"] + g - 1)
                    b = a.take()
                    a.given(f(sgf[:, g % 2, 0:n], b[:, 0:n], ACT.Silu))

            ffn(T, "f0")
            barrier(a, "", 12)
            act.dma_start(swa_c, dram["swa"]).then_inc(S("band_in"), 16)
            norm("n5", sq_b, slice(0, T))
            modulate("n5", slice(0, T), mod2b[:, 0:16])
            copies(8, lambda j: oq[:, j, :])
            copies(1, lambda j: okk)
            copies(1, lambda j: region(2560, 512))
            barrier(a, "", 13)
            attention("swa", swa_items())
            norm("n6", sq_b, LAT, after="res_n6")
            modulate("n6", LAT, mod2b[:, 48:64])
            barrier(a, "", 14)
            ffn(SEQ, "f1")
            norm("n7", sq_b, LAT, after="res_f1")
            modulate("n7", LAT, None)
            for i in range(2):
                for half in range(2):
                    b = a.take()
                    a.given(f(res[:, i, half * 512:(half + 1) * 512], b[:, :], ACT.Copy))
            act.wait_ge(back["act"], a.n_back)
            act.dma_start(out, res).then_inc(S("stored"), 16)
            act.wait_ge(S("stored"), 16)

        @block.vector
        def _(dve):
            v = dve_s
            V = nc.vector
            tt, ts, stt = V.tensor_tensor, V.tensor_scalar, V.scalar_tensor_tensor
            ADD, SUB, MUL, MAX, EQ = ALU.add, ALU.subtract, ALU.mult, ALU.max, ALU.is_equal

            v.does(V.memset(small[:, :], 0.0))
            v.does(V.memset(cond1, 0.0))
            v.does(V.memset(eps_c[:, 0:1], EPS))
            v.signals(V.memset(eps_c[:, 1:2], GN_EPS), "eps_set")
            dve.wait_ge(S("params_in"), 32)

            def modulation(x, m, bias):
                if x and x % KD == 0:
                    g = slice(32 * (x // KD - 1), 32 * (x // KD))
                    b = v.take()[:, :].rearrange("p (c g r) -> p c g r", c=4, g=4)[:, :, :, 0:2]
                    mv_, bv = (z[:, g].rearrange("p (g c x) -> p c g x", c=4, g=4) for z in (m, bias))
                    v.given(tt(mv_, b, bv, ADD))

            def norm(name, cols, m, part, g=None):
                n = cols.stop - cols.start
                late = name == "n1"

                def coefficients():
                    sc = m[:, 16 * part:16 * part + 16]
                    v.does(ts(coef[:, 0:16], sc, 1.0, None, ADD))
                    if g is not None:
                        cv = coef[:, 0:16].rearrange("p (k x) -> p k x", x=2)
                        v.does(tt(cv, cv, g.unsqueeze(2).broadcast_to((P, KD, 2)), MUL))

                if m is not None and not late:
                    coefficients()
                dve.wait_ge(back["act"], marks[name]["act"] + 1)
                v.does(V.reciprocal(rs_t[:, 0:n], rs_t[:, 0:n]))
                if late:
                    for k in range(KD):
                        ins = tt(A[:, k, cols], H[:, k, cols], rs_t[:, 0:n], MUL)
                    v.signals(ins, "root_used")
                    for x in range(ADA + 1):
                        modulation(x, mod1, Q("b_ada", 0, 96))
                    dve.wait_ge(back["dve"], v.n_back)
                    coefficients()
                    v.signals(V.memset(small[:, LM + 5:LM + 6], 0.0), "coef_n1")
                    return
                for k in range(KD):
                    tt(A[:, k, cols], H[:, k, cols], rs_t[:, 0:n], MUL).then_inc(S("scaled_" + name), 1)

            def attention(name, items, extra=None):
                n = len(items)
                for t in range(n + 4):
                    if t < n:
                        it = items[t]
                        b = v.take()
                        nk, s = it["nk"], it["s"]
                        cc = MX + 4 * (t % 4)
                        if it["bias"] is not None:
                            v.does(ts(s[:, 0:CTX], b[:, 0:CTX], it["scale"], None, MUL))
                            v.gives(stt(out=s[:, CTX:T], in0=b[:, CTX:T], scalar=it["scale"], in1=it["bias"],
                                        op0=MUL, op1=ADD))
                        else:
                            v.gives(ts(s[:, 0:nk], b[:, 0:nk], it["scale"], None, MUL))
                        if it["sink"] is not None:
                            v.does(V.tensor_reduce(small[:, cc + 3:cc + 4], s[:, 0:nk], AX, MAX))
                            ts(small[:, cc:cc + 1], small[:, cc + 3:cc + 4], it["sink"], -1.0, MAX, MUL)\
                                .then_inc(S("max_" + name), 1)
                        else:
                            V.tensor_reduce(small[:, cc:cc + 1], s[:, 0:nk], AX, MAX, negate=True)\
                                .then_inc(S("max_" + name), 1)
                    if 0 <= t - 1 < n:
                        it = items[t - 1]
                        nk, p = it["nk"], it["p"]
                        cc = MX + 4 * ((t - 1) % 4)
                        dve.wait_ge(S("exp_" + name), t)
                        den = small[:, cc + 1:cc + 2]
                        inv = small[:, cc + 3:cc + 4]
                        if it["sink"] is not None:
                            v.does(tt(den, den, small[:, cc + 2:cc + 3], ADD))
                        v.does(V.reciprocal(inv, den))
                        if it["comb"] == "second":
                            v.does(tt(inv, inv, neglam, MUL))
                            stt(out=p, in0=p, scalar=inv, in1=it["before"], op0=MUL, op1=ADD)\
                                .then_inc(S("prob_" + name), 1)
                        else:
                            v.signals(ts(p[:, 0:nk], p[:, 0:nk], inv, None, MUL), "prob_" + name) if it["comb"] else \
                                ts(p[:, 0:nk], p[:, 0:nk], inv, None, MUL).then_inc(S("prob_" + name), 1)
                    if 0 <= t - 4 < n and items[t - 4]["pv"] is not None:
                        it = items[t - 4]
                        b = v.take()
                        lo, hi = it["rows"]
                        v.given(V.tensor_copy(it["out"], b[lo:hi, 0:P]))
                dve.wait_ge(back["dve"], v.n_back)

            def rotate(dst, cos, sin, tmp, name=None):
                b = v.take()
                v.gives(tt(tmp, b[:, 0:SEQ], sin, MUL))
                v.does(tt(dst, dst, cos, MUL))
                ins = tt(dst, dst, tmp, ADD)
                v.signals(ins, name) if name else v.does(ins)

            norm("n1", slice(0, T), mod1, 1, Q("norm1_g", 0, 8))
            dve.wait_ge(S("counts_in"), 16)
            for x in range(4):
                v.does(V.memset(pads[x], 0.0))
            for g, w in enumerate(POOL_WINDOWS):
                dve.wait_ge(back["act"], marks["proj1"]["act"] + g + 1)
                v.does(V.tensor_copy(pads[0][:, 16:272], pool_in[:, g, :]))
                src, half, lo, hi = pads[0], 1, 1, 287
                v.does(tt(pads[1][:, 1:288], pads[0][:, 0:287], pads[0][:, 1:288], ADD))
                last = pads[1]
                if w >= 4:
                    v.does(tt(pads[2][:, 2:286], pads[1][:, 1:285], pads[1][:, 3:287], ADD))
                    last = pads[2]
                if w >= 8:
                    v.does(tt(pads[3][:, 4:284], pads[2][:, 2:282], pads[2][:, 6:286], ADD))
                    last = pads[3]
                if w >= 16:
                    v.does(tt(pads[1][:, 8:280], pads[3][:, 4:276], pads[3][:, 12:284], ADD))
                    last = pads[1]
                v.does(tt(w1a[:, g, :], last[:, 16:272], cnt_c[:, g * SEQ:(g + 1) * SEQ], MUL))
                v.signals(tt(w1a[:, g, :], w1a[:, g, :], pool_in[:, g, :], SUB), "pool_diff")
            for g in range(4):
                b = v.take()
                v.given(ts(pool_out[:, g, :], b[:, 0:SEQ], Q("pool_scale", g), None, MUL))
            lq = region(17664, 256).rearrange("p (i n) -> p i n", i=4)
            for x in range(2):
                v.does(tt(pads[0][:, 0:64], lq[:, 2 * x, :], lq[:, 2 * x + 1, :], MUL))
                v.does(V.tensor_reduce(small[:, LM + x:LM + x + 1], pads[0][:, 0:64], AX, ADD))
            v.signals(V.memset(small[:, LM + 5:LM + 6], 0.0), "lam_dots")
            dve.wait_ge(S("lam_exp"), 1)
            v.does(tt(neglam, small[:, LM + 3:LM + 4], small[:, LM + 2:LM + 3], SUB))
            v.does(ts(neglam, neglam, LAM_INIT, None, SUB))
            for x in range(8):
                n = SEQ if x < 4 else T
                src = q_in[:, x, :] if x < 4 else k_in[:, x - 4, :]
                lat = q_in[:, x, :] if x < 4 else k_in[:, x - 4, LAT]
                r = rs2[:, x % 2, 0:n]
                dve.wait_ge(back["act"], marks["qk"]["act"] + x + 1)
                v.does(V.reciprocal(r, r))
                v.signals(stt(out=src, in0=src, scalar=Q("q_norm_g" if x < 4 else "k_norm_g"), in1=r,
                              op0=MUL, op1=MUL), "qk_normed")
                rotate(lat, C("cos64"), C("sin64"), pads[2][:, 0:SEQ], "rotated")
            attention("diff", diff_items())
            v.signals(V.memset(small[:, LM + 5:LM + 6], 0.0), "diff_evac")
            for h in range(4):
                dve.wait_ge(back["act"], marks["diffnorm"]["act"] + h + 1)
                v.does(V.reciprocal(dstd[:, h, :], dstd[:, h, :]))
                v.does(ts(dstd[:, h, :], dstd[:, h, :], Q("subln_g"), 1 - LAM_INIT, MUL, MUL))
                v.does(tt(att_out[:, h, :], w1a[:, h, :], dstd[:, h, :], MUL))
            barrier(v, "", 1)
            v.does(tt(c0t, Q("mu0", 0, 15), Q("mu1", 0, 15), ADD))
            v.does(ts(c0t, c0t, -1.0, 1.0, MUL, ADD))
            for m in range(NRW):
                b = v.take()
                if m < 4:
                    dst, src = u_r[:, m, :], b[:, 0:SEQ]
                elif m == RW_G:
                    dst, src = u_g, b[:, LAT]
                else:
                    dst = (u_k[:, m - 4, :] if m < 8 else u_v[:, m - 8, :] if m < 12 else u_w if m == RW_W else u_a)
                    src = b[:, :]
                v.does(ts(dst, src, c0t[:, m:m + 1], None, MUL))
                ns = dst.free_size() // SEQ
                ds, ss = (z.rearrange("p (s t) -> p s t", s=ns) for z in (dst, src))
                v.does(stt(out=ds[:, :, 1:SEQ], in0=ss[:, :, 0:SEQ - 1], scalar=Q("mu0", m), in1=ds[:, :, 1:SEQ],
                           op0=MUL, op1=ADD))
                v.gives(stt(out=ds[:, :, 0:SEQ - 1], in0=ss[:, :, 1:SEQ], scalar=Q("mu1", m),
                            in1=ds[:, :, 0:SEQ - 1], op0=MUL, op1=ADD))
            v.signals(V.memset(small[:, LM + 5:LM + 6], 0.0), "shifted")
            for jt in range(5):
                if jt < 4:
                    e = e1 if jt % 2 == 0 else e2
                    v.does(ts(KK[:, jt, :], u_k[:, jt, :], Q("k_k", jt), None, MUL))
                    v.signals(tt(e, KK[:, jt, :], KK[:, jt, :], MUL), "kk_sq")
                if jt:
                    dve.wait_ge(back["act"], marks["lora"]["act"] + 20 + jt)
                    r = e3 if jt % 2 == 1 else e4
                    v.does(ts(r, r, 1e-12, None, MAX))
                    v.does(V.reciprocal(r, r))
                    v.does(tt(KK[:, jt - 1, :], KK[:, jt - 1, :], r, MUL))
            v.does(ts(oneka, Q("k_a", 0, 4), -1.0, 1.0, MUL, ADD))
            dve.wait_ge(back["act"], marks["lora"]["act"] + 16)
            for jt in range(4):
                r = RKs[:, jt, :]
                v.does(tt(r, AG[:, jt, LAT], AG[:, 4 + jt, LAT], ADD))
                v.does(ts(r, r, Q("k_a", jt), oneka[:, jt:jt + 1], MUL, ADD))
                v.does(ts(r, r, oneka[:, jt:jt + 1], None, ADD))
                v.does(tt(r, r, u_k[:, jt, LAT], MUL))
                v.does(stt(out=r, in0=r, scalar=Q("r_k", jt), in1=u_r[:, jt, :], op0=MUL, op1=MUL))
            for x in range(8):
                d, jt = divmod(x, 4)
                lw, ag = LW[:, x, :], AG[:, x, :]
                v.does(ts(lw, lw, -math.exp(-0.5), None, MUL))
                v.does(V.tensor_tensor_scan(cumt, C("restart"), lw, 0.0, MUL, ADD))
                c3, l3 = (z.rearrange("p (c n) -> p c n", c=NCH) for z in (cumt, e4))
                v.does(V.tensor_copy(tots[:, x, :], c3[:, :, CH - 1]))
                if d == 0:
                    ins = tt(e4, cumt, lw, SUB)
                else:
                    v.does(tt(l3, tots[:, x, :].unsqueeze(2).broadcast_to((P, NCH, CH)), c3, SUB))
                    ins = tt(cumt, e4, lw, ADD)
                v.signals(ins, "cumulated")
                v.does(ts(lw, ag, Q("k_a", jt), oneka[:, jt:jt + 1], MUL, ADD))
                v.does(tt(lw, lw, u_k[:, jt, :], MUL))
                v.does(tt(ag, ag, KK[:, jt, :], MUL))
                dve.wait_ge(S("exps"), x + 1)
                kk = KK[:, jt, :].rearrange("p (c n) -> p c n", c=NCH)
                ee = e2.rearrange("p (c n) -> p c n", c=NCH)
                stt(out=ARC[:, x, :, :], in0=ee[:, 0:4, :], scalar=-1.0, in1=kk[:, 0:4, :], op0=MUL, op1=MUL)
                stt(out=ARL[:, x, :, 0:64], in0=ee[:, 4:8, :], scalar=-1.0, in1=kk[:, 4:8, :], op0=MUL, op1=MUL)
                tt(ARL[:, x, :, 64:128], e1[:, LAT].rearrange("p (c n) -> p c n", c=4),
                   u_r[:, jt, :].rearrange("p (c n) -> p c n", c=4), MUL)
                tt(ag, ag, e3, MUL)
                v.does(tt(lw, lw, e3, MUL))
            for jt in range(4):
                v.does(V.tensor_copy(rk_t[:, jt, :], RKs[:, jt, :]))
            barrier(v, "", 2)
            v.signals(V.memset(cond2, 0.0), "cond_cleared")
            later = iter(range(2 * ADA + 1))

            def modulate_later():
                x = next(later)
                if x <= ADA:
                    modulation(x, mod2a, Q("mod_b0", 0, 96))
                else:
                    modulation(x - ADA, mod2b, Q("mod_b1", 0, 96))

            for step in range(NCH):
                lat = step >= NCH // 2
                cs = [step, (3 - step) if not lat else (NCH - 1 - (step - 4))]
                two = 128 if lat else 64
                bc = lambda mk: mk.unsqueeze(1).broadcast_to((P, 4, mk.shape[1]))
                j4 = lambda b, n=512: b[:, 0:n].rearrange("p (j n) -> p j n", j=4)
                for d in range(2):
                    w = SC[d]
                    b = v.take()
                    v.gives(tt(w["BM"][:, :, 0:two], j4(b)[:, :, 0:two], bc(C(f"mB{d}")[:, 0:two]), MUL))
                    tt(w["Pt"], w["BM"][:, :, 0:64], bc(C("eye64")), ADD)
                    b = v.take()
                    v.given(tt(w["KM"][:, :, 0:two], j4(b)[:, :, 0:two], bc(C(f"mK{d}")[:, 0:two]), MUL))
                    b = v.take()
                    tt(w["Ad"], j4(b, 256), bc(C(f"mA{d}")[:, 0:64]), MUL)
                    tt(w["Ao"], j4(b, 256), bc(C(f"mA{d}")[:, 64:128]), MUL)
                    v.given(V.tensor_copy(w["bt"], b[:, 256:512].rearrange("p (j n) -> p j n", j=4)))
                dve.wait_ge(back["dve"], v.n_back)
                modulate_later()
                for level in range(1, 6):
                    for d in range(2):
                        b = v.take()
                        v.gives(tt(SC[d]["Pt"], SC[d]["Pt"], j4(b, 256), ADD))
                    modulate_later()
                for d in range(2):
                    w, c = SC[d], cs[d]
                    if lat:
                        b = v.take()
                        y = ysum[:, c - 4, :, :]
                        if step < 6:
                            v.gives(V.tensor_copy(y, j4(b, 256)))
                        else:
                            v.gives(tt(y, y, j4(b, 256), ADD))
                    if step < NCH - 1:
                        b = v.take()
                        dd = dch[:, 4 * d:4 * d + 4, c].unsqueeze(2).broadcast_to((P, 4, 64))
                        if step:
                            v.gives(tt(w["state"], w["state"], j4(b, 256), ADD))
                            v.signals(tt(w["state"], w["state"], dd, MUL), "state_ready")
                        else:
                            v.gives(V.tensor_copy(w["state"], j4(b, 256)))
                            v.signals(tt(w["state"], w["state"], dd, MUL), "state_ready")
            modulate_later()
            y16 = sw[:, 0:1024].rearrange("p (x n) -> p x n", x=16)
            mean, var = small[:, GNC + 16:GNC + 32], small[:, GNC:GNC + 16]
            b16 = lambda z: z.unsqueeze(2).broadcast_to((P, 16, 64))
            v.does(V.tensor_reduce(mean, y16, AX, ADD))
            v.does(ts(mean, mean, 1.0 / 64, None, MUL))
            v.does(tt(y16, y16, b16(mean), SUB))
            v.does(tt(ysq, y16, y16, MUL))
            v.signals(V.tensor_reduce(var, ysq, AX, ADD), "y_var")
            dve.wait_ge(S("y_std"), 1)
            v.does(V.reciprocal(var, var))
            v.signals(tt(y16, y16, b16(var), MUL), "y_normed")
            for half in range(2):
                b = v.take()[:, :].rearrange("p (j t) -> p j t", j=2)
                for x in range(2):
                    jt = 2 * half + x
                    ins = ts(rwo[:, jt, :], b[:, x, :], Q("gn_w", jt), Q("gn_b", jt), MUL, ADD)
                v.gives(ins)
            for jt in range(4):
                b = v.take()
                v.gives(tt(bon[:, 0:SEQ], b[:, 0:SEQ], u_v[:, jt, LAT], MUL))
                v.does(tt(rwo[:, jt, :], rwo[:, jt, :], bon[:, 0:SEQ], ADD))
                v.does(tt(rwo[:, jt, :], rwo[:, jt, :], g_out[:, jt, :], MUL))
            barrier(v, "", 3)
            for m in range(KD):
                for n in range(3):
                    i = 3 * m + n
                    b = v.take()
                    dve.wait_ge(back["act"], marks["merge"]["act"] + i + 1)
                    s_ = sig[:, i % 6, :]
                    v.gives(tt(s_, s_, b[:, 0:SEQ], MUL))
                    if n == 0:
                        ins = V.tensor_copy(merged[:, m, :], s_)
                    else:
                        ins = tt(merged[:, m, :], merged[:, m, :], s_, ADD)
                    v.signals(ins, "branch_mixed")

            def residual(m, part, cols, x=None):
                n = cols.stop - cols.start
                for k in range(KD):
                    b = v.take()
                    if cols.start == 0:
                        c = 16 * part + 2 * k
                        stt(out=H[:, k, 0:CTX], in0=b[:, 0:CTX], scalar=m[:, c + 1:c + 2], in1=H[:, k, 0:CTX],
                            op0=MUL, op1=ADD)
                        v.given(stt(out=H[:, k, LAT], in0=b[:, LAT], scalar=m[:, c:c + 1], in1=H[:, k, LAT],
                                    op0=MUL, op1=ADD))
                    else:
                        c = 16 * part + 2 * k
                        v.given(stt(out=H[:, k, LAT], in0=b[:, 0:SEQ], scalar=m[:, c:c + 1], in1=H[:, k, LAT],
                                    op0=MUL, op1=ADD))
                dve.wait_ge(back["dve"], v.n_back)

            residual(mod1, 2, LAT)
            norm("n2", LAT, mod1, 4, Q("norm2_g", 0, 8))
            barrier(v, "", 4)
            for i in range(2):
                b = v.take()
                v.gives(V.tensor_copy(logit[:, i, :], b[:, 0:36]))
            for i in range(2):
                l8, m8, f8, le8 = r8[:, 0:8], r8[:, 8:16], r8[:, 16:24], r8[:, 24:32]
                oh = r8[:, 32:36]
                v.does(V.memset(l8, -3e38))
                v.does(V.tensor_copy(l8[:, 0:4], logit[:, i, 0:4]))
                v.does(V.max(m8, l8))
                v.does(V.max_index(idx[:, 0:8], m8, l8))
                v.does(V.tensor_copy(f8, idx[:, 0:8]))
                v.does(ts(r8[:, 36:37], f8[:, 0:1], 1.0, None, MUL))
                v.signals(ts(r8[:, 90 + i:91 + i], m8[:, 0:1], -1.0, None, MUL), "group_max")
                v.does(ts(oh, C("iota")[:, 0:4], r8[:, 36:37], None, EQ))
                v.does(ts(le8, logit[:, i, 4:12], oh[:, 0:1], None, MUL))
                for g in range(1, 4):
                    v.does(stt(out=le8, in0=logit[:, i, 4 + 8 * g:12 + 8 * g], scalar=oh[:, g:g + 1], in1=le8,
                               op0=MUL, op1=ADD))
                v.does(V.max(m8, le8))
                v.does(V.max_index(idx[:, 0:8], m8, le8))
                v.does(V.tensor_copy(f8, idx[:, 0:8]))
                v.signals(tt(r8[:, 94 + i:95 + i], m8[:, 1:2], m8[:, 0:1], SUB), "top_two")
                v.does(ts(f8[:, 4:5], r8[:, 36:37], float(EPG), None, MUL))
                v.does(ts(f8[:, 0:2], f8[:, 0:2], f8[:, 4:5], None, ADD))
                dve.wait_ge(S("top_exp"), i + 1)
                ex, pg = r8[:, 96 + i:97 + i], r8[:, 92 + i:93 + i]
                v.does(ts(r8[:, 40:41], ex, 1.0, None, ADD))
                v.does(tt(r8[:, 40:41], r8[:, 40:41], pg, MUL))
                v.does(V.reciprocal(r8[:, 41:42], r8[:, 40:41]))
                v.does(tt(r8[:, 42:43], r8[:, 41:42], ex, MUL))
                o1, o2 = r8[:, 112:144], r8[:, 144:176]
                io = C("iota")[:, 0:32]
                v.does(ts(o1, io, f8[:, 0:1], None, EQ))
                v.does(ts(o2, io, f8[:, 1:2], None, EQ))
                v.does(tt(msk[:, i, :], o1, o2, ADD))
                v.does(ts(gat[:, i, :], o1, r8[:, 41:42], None, MUL))
                v.does(stt(out=gat[:, i, :], in0=o2, scalar=r8[:, 42:43], in1=gat[:, i, :], op0=MUL, op1=ADD))
            v.signals(V.memset(small[:, LM + 5:LM + 6], 0.0), "routed")
            b = v.take()
            cnt_b = b
            v.gives(ts(posm, b[:, 0:64].rearrange("p (i n) -> p i n", i=2), 1.0, None, ADD))
            v.does(tt(posm, posm, msk, MUL))
            v.does(ts(posm, posm, -1.0, None, ADD))
            v.does(V.tensor_copy(lcol[0:NE, 0:1], cnt_b[0:NE, 64:65]))
            v.does(ts(lcol[0:NE, 1:2], lcol[0:NE, 0:1], 0.0, None, ALU.is_gt))
            for x in range(1, SEQ // SLOTS):
                ins = stt(out=lcol[0:NE, 1:2], in0=lcol[0:NE, 0:1], scalar=float(x * SLOTS), in1=lcol[0:NE, 1:2],
                          op0=ALU.is_gt, op1=ADD)
                v.does(ins) if x < SEQ // SLOTS - 1 else v.signals(ins, "counted")
            b = v.take()
            v.gives(V.tensor_copy(lcol[0:NE, 2:3], b[0:NE, 0:1]))
            v.does(tt(lcol[0:NE, 3:4], lcol[0:NE, 2:3], lcol[0:NE, 1:2], ADD))
            v.does(ts(lcol[0:NE, 4:5], lcol[0:NE, 2:3], float(SLOTS), None, MUL))
            v.does(ts(in_item[0:NE, :], C("iota")[0:NE, 0:ITEMS], lcol[0:NE, 2:3], None, ALU.is_ge))
            v.signals(stt(out=in_item[0:NE, :], in0=C("iota")[0:NE, 0:ITEMS], scalar=lcol[0:NE, 3:4],
                          in1=in_item[0:NE, :], op0=ALU.is_lt, op1=MUL), "items_cut")
            v.does(ts(item64, C("iota")[:, 0:ITEMS], float(SLOTS), None, MUL))
            b = v.take()
            v.does(ts(slotT[0:NE, :], b[0:NE, 0:SEQ], lcol[0:NE, 4:5], None, ADD))
            v.gives(V.tensor_copy(gateT[0:NE, :], b[0:NE, SEQ:2 * SEQ]))
            b = v.take()
            v.does(V.memset(picked, -1.0))
            v.does(V.memset(weight, 0.0))
            v.does(tt(picked[:, :, 0:ITEMS], b[:, 0:2 * ITEMS].rearrange("p (i n) -> p i n", i=2),
                      item64.unsqueeze(1).broadcast_to((P, 2, ITEMS)), SUB))
            v.does(V.tensor_copy(weight[:, :, 0:ITEMS], b[:, 2 * ITEMS:4 * ITEMS].rearrange("p (i n) -> p i n", i=2)))
            v.gives(V.tensor_copy(item_expert[0:1, :], b[0:1, 4 * ITEMS:5 * ITEMS]))
            v.signals(V.memset(small[:, LM + 5:LM + 6], 0.0), "listed")
            v.does(V.memset(yacc, 0.0))
            barrier(v, "", 5)
            m = marks["moe"]

            def select(pair):
                for i in range(2):
                    for x in range(2):
                        c = slice(SLOTS * x, SLOTS * (x + 1))
                        at = bass.ds(pair * 2 + x, 1)
                        ts(sel[:, i, c], C("iota"), picked[:, i, at], None, EQ)
                        ins = ts(selg[:, i, c], C("iota"), picked[:, i, at], weight[:, i, at], EQ, MUL)
                ins.then_inc(S("selected"), 1)

            select(0)
            with nc.vector.Fori(0, ITEMS // 2) as it:
                v.it, v.step = it, {"full": m["per"]["n"], "back_act": m["per"]["act"], "back_dve": m["per"]["dve"]}
                b = v.take()
                v.given(V.tensor_copy(pgt, b[:, 0:SEQ]))
                select(it + 1)
                b = v.take()
                dve.wait_ge(back["act"], v.at("back_act", marks["expert"]["act"] + 1))
                v.given(tt(actv, sgl, b[:, :], MUL))
                b = v.take()
                v.given(V.tensor_copy(yex[:, 512:1024], b[:, :]))
                for i in range(2):
                    for half in range(2):
                        b = v.take()
                        y = yacc[:, i, half * 512:(half + 1) * 512]
                        v.given(tt(y, y, b[:, :], ADD))
            v.it = None
            v.n_back += (ITEMS // 2 - 1) * m["per"]["dve"]
            dve.wait_ge(back["dve"], v.n_back)
            for k2 in range(4):
                b = v.take()[:, :].rearrange("p (k t) -> p k t", k=2)
                for x in range(2):
                    k = 2 * k2 + x
                    c = 16 * 5 + 2 * k
                    ins = stt(out=H[:, k, LAT], in0=b[:, x, :], scalar=mod1[:, c:c + 1], in1=H[:, k, LAT],
                              op0=MUL, op1=ADD)
                v.given(ins)
            dve.wait_ge(back["dve"], v.n_back)
            barrier(v, "", 6)

            norm("n3", slice(0, T), mod2a, 1)
            for x in range(4):
                b = v.take()
                v.given(V.tensor_copy(pq[:, x, :] if x < 2 else ckv if x == 2 else krt, b[:, :]))
            barrier(v, "", 7)
            rq, rk = rs_t, osb[:, 7, :]
            dve.wait_ge(back["act"], marks["mla"]["act"] + 1)
            v.does(V.reciprocal(rq[:, :], rq[:, :]))
            for x in range(2):
                v.signals(stt(out=pq[:, x, :], in0=pq[:, x, :], scalar=Q("mla_q_norm", x), in1=rq[:, :],
                              op0=MUL, op1=MUL), "mla_normed")
            dve.wait_ge(back["act"], marks["mla"]["act"] + 2)
            v.does(V.reciprocal(rk, rk))
            v.signals(stt(out=ckv, in0=ckv, scalar=Q("mla_kv_norm"), in1=rk, op0=MUL, op1=MUL), "mla_normed")
            for x in range(6):
                b = v.take()
                v.given(V.tensor_copy(nope[:, x, :] if x < 4 else qr[:, x - 4, :], b[:, :]))
            dve.wait_ge(back["dve"], v.n_back)
            for x in range(3):
                rotate(krt[:, LAT] if x == 2 else qr[:, x, LAT], C("cos32"), C("sin32"), osb[:, 6, 0:SEQ])
            for x in range(4):
                v.signals(ts(kr[:, x, :], krt, C("band")[:, x:x + 1], None, MUL), "kr_banded")
            barrier(v, "", 8)
            attention("mla", mla_items())
            barrier(v, "", 9)
            dve.wait_ge(S("bias_in"), 16)
            attention("na", na_items())
            barrier(v, "", 10)
            residual(mod2a, 2, slice(0, T))
            norm("n4", slice(0, T), mod2a, 4)
            barrier(v, "", 11)

            def ffn(n, name, m):
                for g in range(FT):
                    b = v.take()
                    dve.wait_ge(back["act"], marks[name]["act"] + g + 1)
                    v.given(tt(hid[:, g, 0:n], sgf[:, g % 2, 0:n], b[:, 0:n], MUL))
                residual(m, 5, slice(T - n, T))

            ffn(T, "f0", mod2a)
            barrier(v, "", 12)
            norm("n5", slice(0, T), mod2b, 1)
            dve.wait_ge(back["act"], marks["proj3"]["act"] + 10)
            for x in range(9):
                rotate(okk[:, LAT] if x == 8 else oq[:, x, :], C("cos64"), C("sin64"), rtmp)
            barrier(v, "", 13)
            dve.wait_ge(S("band_in"), 16)
            attention("swa", swa_items())
            residual(mod2b, 2, LAT)
            norm("n6", LAT, mod2b, 4)
            barrier(v, "", 14)
            ffn(SEQ, "f1", mod2b)
            norm("n7", LAT, None, 0)

        @block.sync
        def _(sp):
            w = dram["w"]

            def load(t, src=None):
                s = t % RING
                return sp.dma_start(ring[:, s * TILE:(s + 1) * TILE], w[t] if src is None else src)\
                    .then_inc(ring_full[s], 16)

            def straight(lo, hi):
                for t in range(lo, hi):
                    if t >= RING:
                        sp.wait_ge(full, tile_free[t - RING])
                    load(t, w[t - (ITEMS - NE) * EXP_TILES if t >= PRE else t])

            def expert_of(item):
                return sp.value_load(item_expert[0:1, item], min_val=0, max_val=NE - 1)

            def pair(t0, experts, later=None):
                for i in range(BODY):
                    t = t0 + i
                    sp.wait_ge(full, tile_free[t - RING] if later is None else tile_free[t - RING] + later)
                    load(t, w[bass.ds(experts[i % 2] * EXP_TILES + (PRE + i // 2), 1)].rearrange("a p n -> (a p) n"))

            straight(0, PRE)
            sp.wait_ge(S("listed"), 1)
            per = marks["moe"]["per"]["n"]
            pair(PRE, [expert_of(slice(x, x + 1)) for x in range(2)])
            with nc.sync.Fori(1, ITEMS // 2) as it:
                pair(PRE + BODY, [expert_of(bass.ds(it * 2 + x, 1)) for x in range(2)], (it - 1) * per)
            straight(PRE + ITEMS * EXP_TILES, N_TILES)


def pack(inputs):
    g = {k: np.asarray(v) for k, v in inputs.items()}

    def units(w):
        k, m = w.shape
        return w.reshape(k // P, P, m // P, P).transpose(2, 0, 1, 3).reshape(-1, P, P)

    def wide(w):
        k, n = w.shape
        return w.reshape(k // P, P, n // P, P).transpose(0, 2, 1, 3).reshape(-1, P, P)

    def slabs(w):
        k, m = w.shape
        return w.reshape(k // P, P, m // TILE, UPT, P).transpose(2, 0, 3, 1, 4).reshape(-1, P, P)

    w_in = g["w_in"][0]
    gates, branch = w_in[:, 3968:7040], g["w_br"][0]
    merge = []
    gate_u = [units(gates[:, n * D:(n + 1) * D]).reshape(KD, KD, P, P) for n in range(3)]
    br_u = [units(branch[n]).reshape(KD, JT, P, P) for n in range(3)]
    for m in range(KD):
        for n in range(3):
            merge += [gate_u[n][m], br_u[n][m]]
    parts = [slabs(g["w_ada"][0]), units(w_in[:, 0:1536]), wide(w_in[:, 1536:2048]),
             units(w_in[:, 2048:3968]), np.zeros((KD, P, P), np.float32),
             slabs(g["mod_w_2"][0]), slabs(g["mod_w_2"][1])] + merge + [units(g["w_out"][0])]
    for e in range(NE):
        dn = g["w_exp_down"][0, e]
        parts += [wide(g["w_exp_gate"][0, e]), wide(g["w_exp_up"][0, e]), wide(dn[:, 0:512]), wide(dn[:, 512:1024])]

    def ffn(l):
        gu, out = g["ffn_w_gate_up_2"][l], []
        a, b = (units(z).reshape(FT, KD, P, P) for z in (gu[:, :FF], gu[:, FF:]))
        for f in range(FT):
            out += [a[f], b[f]]
        return out + [units(g["ffn_w_down_2"][l])]

    ev = g["even_w_in_2"][0]
    parts += [units(ev[:, 0:384]), units(np.concatenate([ev[:, 384:416]] * 4, 1)),
              units(ev[:, 416:1440]), wide(ev[:, 1440:1952]), units(g["even_w_out_2"][0])] + ffn(0)
    od = g["odd_w_in_2"][0]
    pair = np.concatenate([np.r_[j * 64:(j + 1) * 64, (j + 8) * 64:(j + 9) * 64] for j in range(8)])
    parts += [units(od[:, pair]), units(od[:, 1024:1152]), wide(od[:, 1152:1280]),
              units(g["odd_w_out_2"][0][pair])] + ffn(1)
    stream = np.concatenate(parts, 0)
    n = PRE + NE * EXP_TILES + POST
    assert stream.shape[0] == n * UPT
    stream = np.ascontiguousarray(stream.reshape(n, UPT, P, P).transpose(0, 2, 1, 3)).reshape(n, P, TILE)

    col = lambda a: a.reshape(-1, P).T
    two = lambda a, b: np.stack([col(a), col(b)], 2).reshape(P, -1)
    rows = lambda a: np.broadcast_to(a.reshape(1, -1), (P, a.size))
    par = {
        "c1": two(g["c"], g["c_ctx"]), "c2": two(g["c_2"], g["c_ctx_2"]), "b_ada": two(g["b_ada"], g["b_ada"]),
        "mod_b0": two(g["mod_b_2"][0], g["mod_b_2"][0]), "mod_b1": two(g["mod_b_2"][1], g["mod_b_2"][1]),
        "norm1_g": col(g["norm1_g"]), "norm2_g": col(g["norm2_g"]), "pool_scale": col(g["pool_scale"]),
        "q_norm_g": col(np.tile(g["q_norm_g"][0], 2)), "k_norm_g": col(np.tile(g["k_norm_g"][0], 2)),
        "subln_g": col(g["subln_g"]), "mu0": col(g["shift_mu"][0, 0]), "mu1": col(g["shift_mu"][0, 1]),
        "w0": col(g["decay_w0"]), "a0": col(g["aaa_a0"]), "k_k": col(g["k_k"]), "k_a": col(g["k_a"]),
        "r_k": col(g["r_k"]), "gn_w": col(g["gn_w"]), "gn_b": col(g["gn_b"]),
        "mla_q_norm": col(g["mla_q_norm_2"]), "mla_kv_norm": col(g["mla_kv_norm_2"]),
        "final_norm": col(g["final_norm_2"]), "sinks": rows(g["swa_sinks_2"]),
    }
    par = np.concatenate([par[n].reshape(P, w) for n, w in PARAM_WIDTHS], 1)
    kcols = lambda w: w.reshape(-1, P, w.shape[1]).transpose(1, 0, 2).reshape(P, -1)
    router = np.concatenate([g["w_router_group"][0], g["w_router_expert"][0]], 1)
    sw1 = np.concatenate([g["pool_w"][0].transpose(1, 0, 2).reshape(P, 512), g["decay_w2"].reshape(P, 512),
                          g["aaa_a2"].reshape(P, 512), g["gate_w2"][0], kcols(router)], 1)
    q_up = g["mla_w_q_up_2"][0].reshape(256, 8, 96)
    q_up = np.concatenate([q_up[:, :, 0:64].reshape(256, 512), q_up[:, :, 64:].reshape(256, 256)], 1)
    uk = g["mla_w_uk_2"][0].transpose(0, 2, 1).reshape(4, P, P).transpose(1, 0, 2).reshape(P, 512)
    uv = g["mla_w_uv_2"][0].transpose(1, 0, 2).reshape(P, 512)
    sw2 = np.concatenate([kcols(q_up), uk, uv], 1)
    xin = np.concatenate([g["ctx"][0], g["x"][0]], 0).reshape(4, P, D).transpose(1, 0, 2).reshape(P, 4 * D)
    xin2 = g["ctx_2"][0].reshape(2, P, D).transpose(1, 0, 2).reshape(P, 2 * D)
    t = np.arange(SEQ)
    qr_, qc = (t // GRID_W)[:, None], (t % GRID_W)[:, None]
    kr_, kc = (t // GRID_W)[None, :], (t % GRID_W)[None, :]
    first = np.clip(qc - 8, 0, GRID_W - 16)
    seen = (kc >= first) & (kc < first + 16)
    bias = g["na_rel_bias_2"][0][:, kr_ - qr_ + 7, np.clip(kc - qc + 15, 0, 30)]
    bias = np.where(seen[None], bias, np.float32(NEG))
    nab = bias.reshape(8, 2, P, SEQ).transpose(2, 0, 1, 3).reshape(P, 4096)
    con = constants()
    return {"w": stream, "par": par, "con": np.concatenate([con[n] for n, _ in CONST_WIDTHS], 1),
            "cnt": np.concatenate([con["cnt"], rows(g["lambda_qk"])], 1), "swa": con["swa"],
            "sw1": sw1, "sw2": sw2, "xin": xin, "xin2": xin2, "nab": nab}


def program(nc, arrays):
    dram = {n: nc.dram_tensor("in_" + n, a.shape, F32, kind="ExternalInput").ap() for n, a in arrays.items()}
    out = nc.dram_tensor("out_0", (SEQ, D), F32, kind="ExternalOutput").ap()
    build(nc, dram, out.rearrange("(i p) n -> p i n", p=P))


def kernel(**inputs):
    import concourse.bacc as bacc
    from concourse.bass_utils import run_bass_kernel_spmd

    arrays = {n: np.ascontiguousarray(a, dtype=np.float32) for n, a in pack(inputs).items()}
    nc = bacc.Bacc("TRN2", target_bir_lowering=False, num_devices=1)
    program(nc, arrays)
    r = run_bass_kernel_spmd(nc, [{"in_" + n: a for n, a in arrays.items()}], core_ids=[0])
    return r.results[0]["out_0"].reshape(1, SEQ, D)
```
